# Optimizing a Trainium2 kernel written in Bass

```python
import math
import jax, jax.numpy as jnp
from jax import lax
import numpy as np

D_MODEL = 1024
BATCH = 1
SEQ = 1024
DEPTH = 1

N_MEM = 256
MEM_HEADS = 4
MEM_HEAD_DIM = D_MODEL // MEM_HEADS
HEAD_DIM = 64
SWA_HEADS = D_MODEL // HEAD_DIM
SWA_KV_HEADS = 4
WINDOW = 128
BLOCK = 128
REL_BUCKETS = 32
REL_MAX_DIST = 128
CONV_WIDTH = D_MODEL
CONV_K = 3
D_FF = 2816
EPS = 1e-6
NEG_INF = -1e30
POS_PAD = 1 << 30

Q_WIDTH = SWA_HEADS * HEAD_DIM
KV_WIDTH = SWA_KV_HEADS * HEAD_DIM
IN_WIDTHS = (Q_WIDTH, KV_WIDTH, KV_WIDTH, CONV_WIDTH, CONV_WIDTH, CONV_WIDTH, D_MODEL, D_MODEL)
IN_WIDTH = Q_WIDTH + 2 * KV_WIDTH + 3 * CONV_WIDTH + 2 * D_MODEL

kernel_name = "hybrid_gated_swa_shortconv_macaron"

def rms_norm(x, g):
    xf = x.astype(jnp.float32)
    y = xf * lax.rsqrt(jnp.mean(xf * xf, axis=-1, keepdims=True) + EPS)
    return (y * g.astype(jnp.float32)).astype(x.dtype)

def swiglu_ffn(h, w_gu, w_down):
    gate, up = jnp.split(h @ w_gu, 2, axis=-1)
    return (jax.nn.silu(gate) * up) @ w_down

def split_cols(t, widths):
    outs, start = [], 0
    for w in widths:
        outs.append(t[..., start:start + w])
        start += w
    return outs

def t5_causal_bucket(rel):
    n = jnp.maximum(rel, 0)
    max_exact = REL_BUCKETS // 2
    nf = jnp.maximum(n, 1).astype(jnp.float32)
    large = max_exact + (jnp.log(nf / max_exact) / math.log(REL_MAX_DIST / max_exact)
                         * (REL_BUCKETS - max_exact)).astype(jnp.int32)
    large = jnp.minimum(large, REL_BUCKETS - 1)
    return jnp.where(n < max_exact, n, large)

def with_prev_block(t, fill):
    b, s = t.shape[0], t.shape[1]
    nb = s // BLOCK
    tb = t.reshape((b, nb, BLOCK) + t.shape[2:])
    pad = jnp.full_like(tb[:, :1], fill)
    prev = jnp.concatenate([pad, tb[:, :-1]], axis=1)
    return jnp.concatenate([prev, tb], axis=2)

def sliding_window_gqa(q, k, v, positions, rel_bias, sinks):
    b, s, _ = q.shape
    nb = s // BLOCK
    grp = SWA_HEADS // SWA_KV_HEADS
    qb = q.reshape(b, nb, BLOCK, SWA_KV_HEADS, grp, HEAD_DIM)
    kb = with_prev_block(k.reshape(b, s, SWA_KV_HEADS, HEAD_DIM), 0)
    vb = with_prev_block(v.reshape(b, s, SWA_KV_HEADS, HEAD_DIM), 0)
    pq = positions.reshape(b, nb, BLOCK)
    pk = with_prev_block(positions, POS_PAD)
    rel = pq[:, :, :, None] - pk[:, :, None, :]
    visible = (rel >= 0) & (rel < WINDOW)
    bias = jnp.moveaxis(rel_bias[t5_causal_bucket(rel)], -1, 2)
    bias = bias.reshape(b, nb, SWA_KV_HEADS, grp, BLOCK, 2 * BLOCK).astype(jnp.float32)
    logits = jnp.einsum('bnqhgd,bnkhd->bnhgqk', qb, kb).astype(jnp.float32) * (HEAD_DIM ** -0.5)
    logits = jnp.where(visible[:, :, None, None], logits + bias, NEG_INF)
    sink = jnp.broadcast_to(sinks.astype(jnp.float32).reshape(1, 1, SWA_KV_HEADS, grp, 1, 1),
                            logits.shape[:-1] + (1,))
    probs = jax.nn.softmax(jnp.concatenate([logits, sink], axis=-1), axis=-1)[..., :-1]
    out = jnp.einsum('bnhgqk,bnkhd->bnqhgd', probs.astype(vb.dtype), vb)
    return out.reshape(b, s, Q_WIDTH)

def short_conv(u, w_conv):
    s = u.shape[1]
    up = jnp.pad(u, ((0, 0), (CONV_K - 1, 0), (0, 0)))
    return sum(w_conv[j] * up[:, j:j + s] for j in range(CONV_K))

def memory_cross_attention(h, mem_h, w_q, w_kv, w_o):
    b, s, _ = h.shape
    m = mem_h.shape[1]
    q = (h @ w_q).reshape(b, s, MEM_HEADS, MEM_HEAD_DIM)
    k, v = jnp.split(mem_h @ w_kv, 2, axis=-1)
    k = k.reshape(b, m, MEM_HEADS, MEM_HEAD_DIM)
    v = v.reshape(b, m, MEM_HEADS, MEM_HEAD_DIM)
    logits = jnp.einsum('bshd,bmhd->bhsm', q, k).astype(jnp.float32) * (MEM_HEAD_DIM ** -0.5)
    probs = jax.nn.softmax(logits, axis=-1)
    o = jnp.einsum('bhsm,bmhd->bshd', probs.astype(v.dtype), v).reshape(b, s, D_MODEL)
    return o @ w_o

def setup_inputs(seed: int = 0) -> dict:
    key = jax.random.key(seed)
    ks = jax.random.split(key, 24)
    f32 = jnp.float32

    def dense(k, shape, fan_in):
        return jax.random.normal(k, shape, f32) * (fan_in ** -0.5)

    def gain(k, shape):
        return 1.0 + 0.05 * jax.random.normal(k, shape, f32)

    L = DEPTH
    x = jax.random.normal(ks[0], (BATCH, SEQ, D_MODEL), f32)
    mem = jax.random.normal(ks[1], (BATCH, N_MEM, D_MODEL), f32)
    offsets = jax.random.randint(ks[2], (BATCH, 1), 0, 1024, dtype=jnp.int32)
    positions = offsets + jnp.arange(SEQ, dtype=jnp.int32)[None, :]
    return {
        "x": x,
        "mem": mem,
        "positions": positions,
        "rel_bias": 0.5 * jax.random.normal(ks[3], (REL_BUCKETS, SWA_HEADS), f32),
        "ffn1_norm": gain(ks[4], (L, D_MODEL)),
        "ffn1_w_gu": dense(ks[5], (L, D_MODEL, 2 * D_FF), D_MODEL),
        "ffn1_w_down": dense(ks[6], (L, D_FF, D_MODEL), D_FF),
        "mix_norm": gain(ks[7], (L, D_MODEL)),
        "w_in": dense(ks[8], (L, D_MODEL, IN_WIDTH), D_MODEL),
        "sinks": 0.5 * jax.random.normal(ks[9], (L, SWA_HEADS), f32),
        "conv_w": dense(ks[10], (L, CONV_K, CONV_WIDTH), CONV_K),
        "w_out": dense(ks[11], (L, D_MODEL, D_MODEL), D_MODEL),
        "xattn_norm": gain(ks[12], (L, D_MODEL)),
        "mem_norm": gain(ks[13], (L, D_MODEL)),
        "xattn_wq": dense(ks[14], (L, D_MODEL, D_MODEL), D_MODEL),
        "xattn_wkv": dense(ks[15], (L, D_MODEL, 2 * D_MODEL), D_MODEL),
        "xattn_wo": dense(ks[16], (L, D_MODEL, D_MODEL), D_MODEL),
        "ffn2_norm": gain(ks[17], (L, D_MODEL)),
        "ffn2_w_gu": dense(ks[18], (L, D_MODEL, 2 * D_FF), D_MODEL),
        "ffn2_w_down": dense(ks[19], (L, D_FF, D_MODEL), D_FF),
        "final_norm": gain(ks[20], (D_MODEL,)),
    }

def reference(x, mem, positions, rel_bias, ffn1_norm, ffn1_w_gu, ffn1_w_down, mix_norm, w_in,
              sinks, conv_w, w_out, xattn_norm, mem_norm, xattn_wq, xattn_wkv, xattn_wo,
              ffn2_norm, ffn2_w_gu, ffn2_w_down, final_norm):
    for l in range(DEPTH):
        x = x + 0.5 * swiglu_ffn(rms_norm(x, ffn1_norm[l]), ffn1_w_gu[l], ffn1_w_down[l])
        h = rms_norm(x, mix_norm[l])
        q, k, v, c_pre, b_post, u, g_attn, g_conv = split_cols(h @ w_in[l], IN_WIDTHS)
        attn = sliding_window_gqa(q, k, v, positions, rel_bias, sinks[l])
        conv = b_post * short_conv(c_pre * u, conv_w[l])
        merged = jax.nn.sigmoid(g_attn) * attn + jax.nn.sigmoid(g_conv) * conv
        x = x + merged @ w_out[l]
        x = x + memory_cross_attention(rms_norm(x, xattn_norm[l]), rms_norm(mem, mem_norm[l]),
                                       xattn_wq[l], xattn_wkv[l], xattn_wo[l])
        x = x + 0.5 * swiglu_ffn(rms_norm(x, ffn2_norm[l]), ffn2_w_gu[l], ffn2_w_down[l])
    return rms_norm(x, final_norm)


_drawn_inputs = setup_inputs


def setup_inputs(seed=0):
    import zlib

    import numpy as np

    out = dict(_drawn_inputs(seed))
    spreads = {}
    factors = {'sinks': 8.0, 'xattn_norm': 8.0, 'mem_norm': 8.0, 'ffn2_norm': 3.254}
    for name, (base, spread) in spreads.items():
        noise = np.random.default_rng([zlib.crc32(name.encode()), seed]).standard_normal(out[name].shape)
        drawn = base * np.exp(spread * noise) if base else spread * noise
        out[name] = __import__('jax').numpy.asarray(drawn.astype(out[name].dtype))
    for name, factor in factors.items():
        out[name] = (out[name] * factor).astype(out[name].dtype)
    return out
```

```python
from contextlib import ExitStack

import numpy as np

import concourse.bass as bass
from concourse import mybir

F32, F32R, I32 = mybir.dt.float32, mybir.dt.float32r, mybir.dt.int32
ALU, ACT, AX = mybir.AluOpType, mybir.ActivationFunctionType, mybir.AxisListType

P = 128
D, S, F, M = 1024, 1024, 2816, 256
HALF = 512
DT, FT, NB = D // P, F // P, S // P
HEADS, KVH, HD = 16, 4, 64
MEM_HEADS, MHD = 4, 256
BUCKETS, MAX_DIST, WINDOW = 32, 128, 128
EPS, NEG_INF = 1e-6, -1e30

RUN = 384
ROWLEN = HEADS * RUN
REGION = P * ROWLEN + P * 3
POS_PAD = 1 << 30
POS_HIGH = 1 << 16
POS_ROW = P + S

KV_BLOCKS, FFN_BLOCKS, QKV_BLOCKS, CONV_BLOCKS, Q_BLOCKS, O_BLOCKS = 16, 3 * FT, 12, 48, 8, 8
KV0 = 0
FFN1 = KV0 + KV_BLOCKS
QKV0 = FFN1 + FFN_BLOCKS
CONV0 = QKV0 + QKV_BLOCKS
Q0 = CONV0 + CONV_BLOCKS
O0 = Q0 + Q_BLOCKS
FFN2 = O0 + O_BLOCKS
BLOCKS = FFN2 + FFN_BLOCKS

FFN1_D, CONV_D, O_D, FFN2_D = 0, FT, FT + DT, FT + 2 * DT
FFN1_T, CONV_T, FFN2_T = 0, FT, FT + DT
KV_A, FFN1_A, QKV_A, CONV_A, Q_A, FFN2_A = 0, 8, 30, 36, 60, 64
KV_B, FFN1_B, QKV_B, CONV_B, Q_B, FFN2_B = 0, 8, 30, 36, 52, 56

CREDIT = 32

POS_STEPS = 18


def need(eng, sem, n):
    if isinstance(n, int) and n <= 0:
        return
    eng.wait_ge(sem, n + CREDIT)


def stand(eng, passed):
    eng.sem_inc(passed, 1)


def hs(h):
    return slice(h * HALF, (h + 1) * HALF)


def build(nc, xT, memT, weights, gains, conv_w, table, onehot, sinks, positions, out):
    with ExitStack() as ctx:
        def sb(name, shape, dt=F32):
            return ctx.enter_context(nc.sbuf_tensor(name, shape, dt))

        def psum(name, shape):
            return ctx.enter_context(nc.psum_tensor(name, shape, F32))

        def sem(name):
            return ctx.enter_context(nc.semaphore(name))

        def overlay(*groups):
            found, biggest = [], max(groups, key=lambda g: sum(int(np.prod(s[1:])) for _, s, _ in g))
            for g in groups:
                if g is not biggest:
                    with ExitStack() as inner:
                        found += [inner.enter_context(nc.sbuf_tensor(*t)) for t in g]
            found += [ctx.enter_context(nc.sbuf_tensor(*t)) for t in biggest]
            byname = {t.name: t for t in found}
            return [byname[n] for g in groups for n, _, _ in g]

        h = sb("h", [P, 2, DT, S], F32R)
        x, kz, vv, qs, pt = overlay(
            [("x", [P, DT, S], F32)],
            [("kz", [P, 2, 2, 2, 2, P], F32R),
             ("vv", [P, 2, 2, 256], F32R),
             ("qs", [P, 2, DT, P], F32R),
             ("pt", [P, 2, 2, 2, 256], F32R)])
        qkv = sb("qkv", [P, QKV_BLOCKS, S])
        wsp = sb("wsp", [P, 2, 2, 1024], F32R)
        raw = sb("raw", [P, 2, 1024])
        rstd = sb("rstd", [P, S])
        sq = sb("sq", [P, 2, HALF])
        memh, act, gate, up, bias, sc, vst, mrg, cu, cv, kx, vx, qx, sx, px = overlay(
            [("memh", [P, 2, DT, M], F32R)],
            [("act", [P, 2, S], F32R), ("gate", [P, S], F32), ("up", [P, S], F32)],
            [("bias", [P, 4, HALF], F32),
             ("sc", [P, 4, HALF], F32),
             ("vst", [P, 2, P], F32)],
            [("mrg", [P, 2, S], F32R), ("cu", [P, S + 2], F32), ("cv", [P, S], F32)],
            [("kx", [P, 2, 2, M], F32R), ("vx", [P, 2, 2, MHD], F32R), ("qx", [P, 2, 2, 2, 256], F32R),
             ("sx", [P, 2, HALF], F32), ("px", [P, 2, 2, 2, 256], F32R)])
        gn = sb("gn", [P, 6, DT])
        cw = sb("cw", [P, DT, 3])
        ident = sb("ident", [P, P])
        ones = sb("ones", [P, P])
        snk = sb("snk", [P, HEADS])
        nsnk = sb("nsnk", [P, HEADS])
        tab = sb("tab", [BUCKETS + 1, HEADS])
        epst = sb("epst", [P, 1])
        nmx = sb("nmx", [P, 4, 2])
        nm = sb("nm", [P, 4, 2])
        sk = sb("sk", [P, 4, 2])
        esk = sb("esk", [P, 4, 2])
        rs = sb("rs", [P, 4, 2])
        den = sb("den", [P, 4, 2])
        rden = sb("rden", [P, 4, 2])
        hot = qkv[0:BUCKETS + 1, 6, 0:RUN]
        vrow = qkv[0:HEADS, 7, 0:RUN]
        negt = qkv[:, 8, 0:P]
        ipos = qkv[0:1, 2, :].bitcast(I32)
        ihalf = qkv[0:1, 3:5, :].bitcast(I32)
        fpos = (qkv[0:1, 6, :], qkv[0:1, 11, :])
        fpad = (qkv[0:1, 8, P:2 * P], qkv[0:1, 8, 2 * P:3 * P])
        fdiff = qkv[0:1, 3:5, 0:S - 1]
        odd = sb("odd", [1, 4])
        steps = sb("steps", [1, NB])
        flags = sb("flags", [1, 1 + NB], I32)
        mem = qkv[:, 4:6, :].rearrange("p a (b m) -> p (a b) m", m=M)
        kvT = qkv[:, 0:4, :].rearrange("p a (b m) -> p (a b) m", m=M)
        vnat = qkv[:, 9:11, :]
        kmem = qkv[:, 8:10, :].rearrange("p a (b m) -> p (a b) m", m=M)
        vmem = qkv[:, 10:12, :]
        cC, cB, cG, cA = (qkv[:, 8 + n, :] for n in range(4))

        acc = x[:, 0:4, :].rearrange("p a (b k) -> p (a b) k", k=2 * P)
        prod = x[:, 4:8, :].rearrange("p a (b k) -> p (a b) k", k=2 * P)
        krow = bias[:, 0, :].rearrange("p (c k) -> p c k", c=2)
        rel, hit = bias[:, 1, 0:2 * P], bias[:, 1, 2 * P:4 * P]
        bkt, one_of = bias[:, 2, 0:2 * P], bias[:, 2, 2 * P:4 * P]
        qcol = bias[:, 3, 0:2]
        trow = sc[:, 0:2, :].rearrange("p a k -> p (a k)")

        def square(bi, half, k):
            return sq[:, k % 2, :] if bi == 0 else qkv[:, k, hs(half)]

        psA = psum("psA", [P, 2, HALF])
        psB = psum("psB", [P, 2, HALF])
        psD = psum("psD", [P, 4, HALF])

        def psS(n):
            return psA[:, n % 4, :] if n % 4 < 2 else psB[:, n % 4 - 2, :]

        def psT(n):
            return psD[:, n % 2, :]

        def psO(n):
            return psD[:, 2 + n % 2, :]

        bias_dram = nc.dram_tensor("bias_dram", (NB * REGION,), F32)
        vrow_dram = nc.dram_tensor("vrow_dram", (ROWLEN,), F32)
        kv_dram = nc.dram_tensor("kv_dram", (P, 4, 1024), F32)
        x_dram = nc.dram_tensor("x_dram", (P, DT, S), F32)
        pos_dram = nc.dram_tensor("pos_dram", (2 * POS_ROW,), F32)

        const_in = sem("const_in")
        mem_in = sem("mem_in")
        x_in = sem("x_in")
        out_done = sem("out_done")
        tab_in = sem("tab_in")
        vrow_out = sem("vrow_out")
        bias_made = sem("bias_made")
        pos_in = sem("pos_in")
        pos_halves = sem("pos_halves")
        pos_saved = sem("pos_saved")
        rows_in = sem("rows_in")
        region_out = sem("region_out")
        gen = sem("gen")
        tables_done = sem("tables_done")
        kv_saved, kv_back = sem("kv_saved"), sem("kv_back")
        x_saved, x_back = sem("x_saved"), sem("x_back")
        raw_in = [sem("raw_in0"), sem("raw_in1")]
        bias_in = [sem(f"bias_in{n}") for n in range(4)]
        setup = sem("setup")
        vec_setup = sem("vec_setup")
        vrow_mm, vrow_cp = sem("vrow_mm"), sem("vrow_cp")

        counted = {}

        def csem(name, engine):
            s = sem(name)
            counted.setdefault(engine, []).append(s)
            return s

        w_high = csem("w_high", "pool")
        w_ready = csem("w_ready", "pool")
        half_done = csem("half_done", "pe")
        d_full = csem("d_full", "pe")
        ss_full = csem("ss_full", "pe")
        a_read, b_read = csem("a_read", "dve"), csem("b_read", "dve")
        x_added = csem("x_added", "dve")
        h_high = csem("h_high", "act")
        h_low = csem("h_low", "dve")
        sq_made = csem("sq_made", "act")
        root = csem("root", "act")
        rstd_made = csem("rstd_made", "dve")
        silu_done = csem("silu_done", "act")
        act_mid = csem("act_mid", "dve")
        act_high = csem("act_high", "act")
        act_low = csem("act_low", "dve")
        qs_high, qs_low = csem("qs_high", "act"), csem("qs_low", "dve")
        kz_high, kz_low = csem("kz_high", "act"), csem("kz_low", "dve")
        vst_made = csem("vst_made", "act")
        v_turned = csem("v_turned", "pe")
        vv_high, vv_low = csem("vv_high", "act"), csem("vv_low", "dve")
        qk_done = csem("qk_done", "pe")
        scored = csem("scored", "dve")
        maxed = csem("maxed", "dve")
        shifted = csem("shifted", "dve")
        sunk = csem("sunk", "dve")
        exp_done = csem("exp_done", "act")
        summed = csem("summed", "dve")
        inverted = csem("inverted", "dve")
        normed = csem("normed", "pool")
        turned = csem("turned", "pe")
        pt_high, pt_low = csem("pt_high", "act"), csem("pt_low", "dve")
        pv_done = csem("pv_done", "pe")
        o_out = csem("o_out", "act")
        conv_v = csem("conv_v", "dve")
        conv_s = csem("conv_s", "act")
        xo_high, xo_low = csem("xo_high", "act"), csem("xo_low", "dve")
        act_passed, pool_passed = sem("act_passed"), sem("pool_passed")
        m_high, m_low = sem("m_high"), sem("m_low")
        m_sq, m_ss, m_root, m_rstd = sem("m_sq"), sem("m_ss"), sem("m_root"), sem("m_rstd")
        m_turned, m_copied = sem("m_turned"), sem("m_copied")
        outs = sem("outs")
        kxs, kxl = csem("kxs", "act"), csem("kxl", "dve")

        def credits(eng, name):
            for s in counted[name]:
                eng.sem_inc(s, CREDIT)

        def region(r, q0, nq, extra, dims):
            return bass.AP(bias_dram, r * REGION + q0 * ROWLEN + extra, [[ROWLEN, nq], *dims])

        block = ctx.enter_context(nc.Block())

        @block.sync
        def _(sp):
            def fetch(n, s):
                sp.dma_start(raw[:, s, :], weights[n, :, :] if isinstance(n, int)
                             else weights[bass.ds(n, 1), :, :].rearrange("a p n -> p (a n)")).then_inc(raw_in[s], 16)

            fetch(0, 0)
            fetch(1, 1)
            with sp.Fori(1, CONV0 // 2 + 1) as i:
                for s in range(2):
                    need(sp, w_ready, 2 * i + s - 1)
                    fetch(2 * i + s, s)

            sp.wait_ge(tables_done, 1)

            def bias_unit(r, par, j, u):
                need(sp, scored, u - 3)
                dst = bias[:, j % 4, :].rearrange("p (h s k) -> p h s k", h=2, s=2)
                for half in range(2):
                    slot = 1 - par if half == 0 else par
                    sp.dma_start(dst[:, :, slot, :], region(r, 0, P, 2 * j * RUN + P + half * P, [[RUN, 2], [1, P]])
                                 ).then_inc(bias_in[j % 4], 16)

            for j in range(8):
                bias_unit(0, 0, j, j)
            for j in range(8):
                bias_unit(1, 1, j, 8 + j)
            with sp.Fori(1, NB // 2) as i:
                for par in range(2):
                    r = sp.value_load(flags[0:1, bass.ds(1 + 2 * i + par, 1)], min_val=1, max_val=NB - 1)
                    for j in range(8):
                        bias_unit(r, par, j, 16 * i + 8 * par + j)

            with sp.Fori(CONV0 // 2 + 1, BLOCKS // 2) as i:
                for s in range(2):
                    need(sp, w_ready, 2 * i + s - 1)
                    fetch(2 * i + s, s)

        @block.gpsimd
        def _(pool):
            credits(pool, "pool")
            pool.memset(ident[:, :], 0.0).then_inc(setup, 1)
            pool.memset(ones[:, :], 1.0).then_inc(setup, 1)
            pool.memset(negt, NEG_INF).then_inc(setup, 1)
            pool.wait_ge(setup, 3)
            pool.affine_select(out=ident[:, :], in_=ident[:, :], compare_op=ALU.not_equal, fill=1.0,
                               base=0, pattern=[[-1, P]], channel_multiplier=1).then_inc(setup, 1)

            def split(n, s, i):
                pool.wait_ge(raw_in[s], 16 * (i + 1))
                need(pool, half_done, 2 * n - 2)
                stand(pool, pool_passed)
                pool.tensor_scalar(wsp[:, s, 0, :], raw[:, s, :], 1.0, 0.0, ALU.mult, ALU.add).then_inc(w_high, 1)
                need(pool, w_high, n + 1)
                pool.tensor_tensor(wsp[:, s, 1, :], raw[:, s, :], wsp[:, s, 0, :].bitcast(F32),
                                   ALU.subtract).then_inc(w_ready, 1)

            def normalise(t, ring, u):
                need(pool, inverted, u + 1)
                stand(pool, pool_passed)
                for hh in range(2):
                    part = t[:, hh * 256:(hh + 1) * 256]
                    ins = pool.tensor_scalar(part, part, rden[:, ring, hh:hh + 1], 0.0, ALU.mult, ALU.add)
                ins.then_inc(normed, 1)

            with pool.Fori(0, CONV0 // 2 + 1) as i:
                for s in range(2):
                    split(2 * i + s, s, i)

            THRESHOLDS = STARTS[1:] + [WINDOW]
            HEAD_STEPS = 4 * (BUCKETS + 1)
            BLOCK_STEPS = 8 + 2 * len(THRESHOLDS) + HEAD_STEPS

            def general_bias(b):
                base = 1 + BLOCK_STEPS * b
                n = 0

                def step(ins):
                    nonlocal n
                    n += 1
                    ins.then_inc(gen, 1)
                    pool.wait_ge(gen, base + n)
                    stand(pool, pool_passed)

                pool.dma_start(krow, bass.AP(pos_dram, b * P, [[0, P], [POS_ROW, 2], [1, 2 * P]])
                               ).then_inc(rows_in, 16)
                with nc.allow_non_contiguous_dma(reason="a position per partition"):
                    pool.dma_start(qcol, bass.AP(pos_dram, P + b * P, [[1, P], [POS_ROW, 2]])).then_inc(rows_in, 16)
                pool.wait_ge(rows_in, 16 + 32 * (b + 1))
                stand(pool, pool_passed)
                for c, part in enumerate((rel, hit)):
                    step(pool.tensor_scalar(part, krow[:, c, :], qcol[:, c:c + 1], -1.0, ALU.subtract, ALU.mult))
                step(pool.tensor_scalar(bkt, rel, -0.5 * POS_HIGH, float(POS_HIGH), ALU.is_lt, ALU.mult))
                step(pool.tensor_tensor(rel, rel, bkt, ALU.add))
                step(pool.tensor_scalar(rel, rel, float(POS_HIGH), 0.0, ALU.mult, ALU.add))
                step(pool.tensor_tensor(rel, rel, hit, ALU.add))
                step(pool.tensor_scalar(bkt, rel, 0.0, float(BUCKETS), ALU.is_lt, ALU.mult))
                for start in THRESHOLDS:
                    step(pool.tensor_scalar(hit, rel, float(start), 1.0, ALU.is_ge, ALU.mult))
                    step(pool.tensor_tensor(bkt, bkt, hit, ALU.add))
                step(pool.memset(acc, 0.0))
                with pool.Fori(0, BUCKETS + 1) as r:
                    at = base + n + 4 * r
                    pool.tensor_scalar(one_of, bkt, 0.0, 1.0, ALU.is_equal, ALU.mult).then_inc(gen, 1)
                    pool.wait_ge(gen, at + 1)
                    stand(pool, pool_passed)
                    pool.tensor_tensor(prod, one_of.rearrange("p (a k) -> p a k", a=1).to_broadcast([P, HEADS, 2 * P]),
                                       trow[:, bass.ds(r * HEADS, HEADS)].rearrange("p (h a) -> p h a", a=1)
                                       .to_broadcast([P, HEADS, 2 * P]), ALU.mult).then_inc(gen, 1)
                    pool.wait_ge(gen, at + 2)
                    pool.tensor_tensor(acc, acc, prod, ALU.add).then_inc(gen, 1)
                    pool.tensor_scalar(bkt, bkt, -1.0, 0.0, ALU.add, ALU.add).then_inc(gen, 1)
                    pool.wait_ge(gen, at + 4)
                    stand(pool, pool_passed)
                n += HEAD_STEPS
                pool.wait_ge(gen, base + n)
                pool.dma_start(region(b, 0, P, P, [[RUN, HEADS], [1, 2 * P]]), acc).then_inc(region_out, 16)
                pool.wait_ge(region_out, 16 * (b + 1))
                stand(pool, pool_passed)

            pool.wait_ge(pos_halves, POS_STEPS)
            pool.wait_ge(bias_made, 16 * 6)
            pool.wait_ge(pos_saved, 16 * 4)
            pool.wait_ge(x_saved, 16)
            need(pool, h_low, 32)
            with pool.If(pool.value_load(flags[0:1, 0:1], min_val=0, max_val=1) > 0):
                pool.memset(trow[:, BUCKETS * HEADS:(BUCKETS + 1) * HEADS], NEG_INF).then_inc(gen, 1)
                pool.dma_start(trow[:, 0:BUCKETS * HEADS], bass.AP(table.tensor, 0, [[0, P], [1, BUCKETS * HEADS]])
                               ).then_inc(rows_in, 16)
                with pool.Fori(0, NB) as b:
                    general_bias(b)
                pool.sem_inc(tables_done, 1)
            with pool.Else():
                pool.sem_inc(tables_done, 1)
            with pool.Fori(0, NB) as b:
                for j in range(8):
                    normalise(sc[:, j % 4, :], j % 4, 8 * b + j)
            with pool.Fori(CONV0 // 2 + 1, O0 // 2 + 1) as i:
                for s in range(2):
                    split(2 * i + s, s, i)
            with pool.Fori(0, MEM_HEADS) as hd:
                for v in range(4):
                    normalise(sx[:, v % 2, :], v, 64 + 4 * hd + v)
                for s in range(2):
                    split(O0 + 2 + 2 * hd + s, s, O0 // 2 + 1 + hd)
            with pool.Fori(FFN2 // 2 + 1, BLOCKS // 2) as i:
                for s in range(2):
                    split(2 * i + s, s, i)

        @block.tensor
        def _(pe):
            credits(pe, "pe")

            def three(o, lhs, rhs, start, stop):
                pe.matmul(o, lhs[0], rhs[0], start=start, stop=False)
                pe.matmul(o, lhs[0], rhs[1], start=False, stop=False)
                return pe.matmul(o, lhs[1], rhs[0], start=False, stop=stop)

            def wtile(n, m):
                s = n % 2
                return [wsp[:, s, part, m * P:(m + 1) * P] for part in range(2)]

            def column(n, s, bank, read, use, first=None):
                need(pe, w_ready, n + 1)
                for half in range(2):
                    need(pe, read, 2 * use + half - 1)
                    for k in range(DT):
                        if first is not None:
                            first(half, k)
                        ins = three(bank[:, half, :], wtile(s, k), [h[:, part, k, hs(half)] for part in range(2)],
                                    k == 0, k == DT - 1)
                    ins.then_inc(half_done, 1)

            def rows(n, s, dn, rhs, ready=None):
                need(pe, w_ready, n + 1)
                for r in range(16):
                    half, m = r // 8, r % 8
                    if ready is not None and m == 0:
                        ready(half)
                    need(pe, x_added, 16 * dn + r - 3)
                    ins = three(psD[:, r % 4, :], wtile(s, m), rhs(half), True, True)
                    ins.then_inc(half_done if m == 7 else d_full, 1)

            def boundary(bi):
                def first(half, k):
                    r = 16 * bi + 8 * half + k
                    need(pe, h_low, r + 1)
                    squares(bi, half, k)
                return first

            def squares(bi, half, k):
                r = 16 * bi + 8 * half + k
                need(pe, sq_made, r + 1)
                pe.matmul(psB[:, half, :], ones[:, :], square(bi, half, k), start=(k == 0), stop=(k == DT - 1)
                          ).then_inc(ss_full, 1)

            pe.wait_ge(tab_in, 32)
            pe.wait_ge(vec_setup, 1)
            pe.matmul(psD[0:HEADS, 0, 0:RUN], tab[:, :], hot, start=True, stop=True).then_inc(vrow_mm, 1)

            pe.wait_ge(setup, 4)
            for k in range(DT):
                pe.wait_ge(m_sq, k + 1)
                pe.matmul(psD[:, 1, 0:M], ones[:, :], sq[:, k % 2, 0:M], start=(k == 0), stop=(k == DT - 1)
                          ).then_inc(m_ss, 1)
            pe.wait_ge(m_low, DT)

            def kv_block(n, s, bank, read, use):
                need(pe, w_ready, n + 1)
                need(pe, read, use)
                for k in range(DT):
                    ins = three(bank[:, 0, 0:M], wtile(s, k), [memh[:, part, k, :] for part in range(2)],
                                k == 0, k == DT - 1)
                ins.then_inc(half_done, 2)

            with pe.Fori(0, KV_BLOCKS // 2) as i:
                kv_block(2 * i, 0, psA, a_read, i)
                kv_block(2 * i + 1, 1, psB, b_read, i)
            need(pe, a_read, 8)
            need(pe, b_read, 8)
            for t in range(DT):
                for mt in range(2):
                    n = 2 * t + mt
                    if n >= 2:
                        pe.wait_ge(m_copied, n - 1)
                    pe.transpose(psD[:, 2 + n % 2, 0:P], kvT[:, DT + t, mt * P:(mt + 1) * P], ident[:, :]
                                 ).then_inc(m_turned, 1)

            def use_a(u):
                return u - 4

            def use_b(u):
                return u - 4

            def ffn(n0, a0, b0, d0, bi):
                def act_rhs(half):
                    return [act[:, part, hs(half)] for part in range(2)]

                def act_ready(t):
                    def wait(half):
                        need(pe, act_low, 2 * t + half + 1)
                    return wait

                t0 = FFN1_T if bi == 0 else FFN2_T
                column(n0, n0, psA, a_read, use_a(a0), first=boundary(bi))
                need(pe, root, 2 * bi + 2)
                column(n0 + 1, n0 + 1, psB, b_read, use_b(b0))

                def body(t, n, s):
                    column(n, s, psA, a_read, use_a(a0) + t)
                    rows(n + 1, s + 1, d0 + t - 1, act_rhs, act_ready(t0 + t - 1))
                    column(n + 2, s, psB, b_read, use_b(b0) + t)

                with pe.Fori(0, (FT - 2) // 2) as i:
                    body(2 * i + 1, n0 + 2 + 6 * i, n0)
                    body(2 * i + 2, n0 + 5 + 6 * i, n0 + 1)
                body(FT - 1, n0 + 2 + 3 * (FT - 2), n0)
                rows(n0 + 3 * FT - 1, n0 + 1, d0 + FT - 1, act_rhs, act_ready(t0 + FT - 1))

            pe.wait_ge(m_root, 1)
            pe.wait_ge(m_copied, 16)
            pe.wait_ge(vrow_cp, 1)
            ffn(FFN1, FFN1_A, FFN1_B, FFN1_D, 0)

            need(pe, b_read, 2 * use_b(QKV_B))
            column(QKV0, 0, psA, a_read, use_a(QKV_A), first=boundary(1))
            need(pe, root, 4)
            column(QKV0 + 1, 1, psB, b_read, use_b(QKV_B))
            with pe.Fori(1, QKV_BLOCKS // 2) as i:
                column(QKV0 + 2 * i, 0, psA, a_read, use_a(QKV_A) + i)
                column(QKV0 + 2 * i + 1, 1, psB, b_read, use_b(QKV_B) + i)

            need(pe, a_read, 2 * use_a(CONV_A))
            need(pe, b_read, 2 * use_b(CONV_B))
            need(pe, x_added, 16 * CONV_D)

            def swa_block(b, par):
                need(pe, vst_made, b + 1)
                need(pe, o_out, 8 * b)
                for pr in range(2):
                    ins = pe.transpose(psO(1)[:, pr * P:(pr + 1) * P], vst[:, pr, :], ident[:, :])
                ins.then_inc(v_turned, 1)
                need(pe, qs_low, b + 1)
                need(pe, kz_low, 2 * b + 2)

                def qk(j):
                    need(pe, scored, 8 * b + j - 3)
                    pr = j // 4
                    three(psS(j), [qs[:, part, j, :] for part in range(2)],
                          [kz[:, part, pr, :, :, :].rearrange("p g s k -> p (g s k)") for part in range(2)],
                          True, True).then_inc(qk_done, 1)

                def turn(j):
                    need(pe, normed, 8 * b + j + 1)
                    need(pe, pt_low, 8 * b + j - 1)
                    for slot in range(2):
                        for hh in range(2):
                            ins = pe.transpose(psT(j)[:, slot * 256 + hh * P:slot * 256 + (hh + 1) * P],
                                               sc[:, j % 4, hh * 256 + slot * P:hh * 256 + (slot + 1) * P], ident[:, :])
                    ins.then_inc(turned, 1)

                def pv(j):
                    need(pe, pt_low, 8 * b + j + 1)
                    need(pe, vv_low, b + 1)
                    need(pe, o_out, 8 * b + j - 1)
                    pr = j // 4
                    for slot in range(2):
                        ins = three(psO(j)[:, 0:256], [vv[:, part, slot, pr * P:(pr + 1) * P] for part in range(2)],
                                    [pt[:, j % 2, part, slot, :] for part in range(2)], slot == 0, slot == 1)
                    ins.then_inc(pv_done, 1)

                qk(0)
                qk(1)
                for j in range(10):
                    if j + 2 < 8:
                        qk(j + 2)
                    if 0 <= j - 0 < 8:
                        turn(j)
                    if 0 <= j - 1 < 8:
                        pv(j - 1)

            with pe.Fori(0, NB // 2) as i:
                for par in range(2):
                    swa_block(2 * i + par, par)

            need(pe, scored, 64)
            need(pe, o_out, 64)

            def mrg_rhs(half):
                return [mrg[:, part, hs(half)] for part in range(2)]

            def mrg_ready(t):
                def wait(half):
                    need(pe, act_low, 2 * (CONV_T + t) + half + 1)
                return wait

            A, B = use_a(CONV_A), use_b(CONV_B)

            def conv_tile(t, n, s, peeled):
                column(n, s, psA, a_read, A + 3 * t)
                column(n + 1, s + 1, psB, b_read, B + 2 * t)
                k = 2
                if not peeled:
                    rows(n + 2, s, CONV_D + t - 1, mrg_rhs, mrg_ready(t - 1))
                    k = 3
                column(n + k, s + k, psA, a_read, A + 3 * t + 1)
                column(n + k + 1, s + k + 1, psB, b_read, B + 2 * t + 1)
                column(n + k + 2, s + k + 2, psA, a_read, A + 3 * t + 2)

            conv_tile(0, CONV0, CONV0, True)
            with pe.Fori(1, DT) as t:
                conv_tile(t, CONV0 - 1 + 6 * t, CONV0 + 5, False)
            rows(Q0 - 1, Q0 - 1, CONV_D + DT - 1, mrg_rhs, mrg_ready(DT - 1))

            need(pe, b_read, 2 * use_b(Q_B))
            column(Q0, 0, psA, a_read, use_a(Q_A), first=boundary(2))
            need(pe, root, 6)
            column(Q0 + 1, 1, psB, b_read, use_b(Q_B))
            with pe.Fori(1, Q_BLOCKS // 2) as i:
                column(Q0 + 2 * i, 0, psA, a_read, use_a(Q_A) + i)
                column(Q0 + 2 * i + 1, 1, psB, b_read, use_b(Q_B) + i)
            need(pe, a_read, 2 * use_a(FFN2_A))
            need(pe, b_read, 2 * use_b(FFN2_B))

            def xattn_head(hd):
                need(pe, x_added, 16 * (O_D + 2 * hd))
                need(pe, kxl, 2 * hd + 2)

                def qk(v):
                    u = 64 + 4 * hd + v
                    need(pe, qs_low, NB + 4 * hd + v + 1)
                    need(pe, scored, u - 3)
                    for qb in range(2):
                        for kt in range(2):
                            ins = three(psS(v)[:, qb * 256:(qb + 1) * 256],
                                        [qx[:, v % 2, part, kt, qb * P:(qb + 1) * P] for part in range(2)],
                                        [kx[:, part, kt, :] for part in range(2)], kt == 0, kt == 1)
                    ins.then_inc(qk_done, 1)

                def turn(v):
                    u = 64 + 4 * hd + v
                    need(pe, normed, u + 1)
                    need(pe, pt_low, u - 1)
                    for mt in range(2):
                        for qb in range(2):
                            ins = pe.transpose(psT(v)[:, mt * 256 + qb * P:mt * 256 + (qb + 1) * P],
                                               sx[:, v % 2, qb * 256 + mt * P:qb * 256 + (mt + 1) * P], ident[:, :])
                    ins.then_inc(turned, 1)

                def pv(v):
                    u = 64 + 4 * hd + v
                    need(pe, pt_low, u + 1)
                    need(pe, xo_low, 4 * hd + v - 1)
                    for dt in range(2):
                        for mt in range(2):
                            ins = three(psO(v)[:, dt * 256:(dt + 1) * 256],
                                        [vx[:, part, mt, dt * P:(dt + 1) * P] for part in range(2)],
                                        [px[:, v % 2, part, mt, :] for part in range(2)], mt == 0, mt == 1)
                    ins.then_inc(pv_done, 1)

                qk(0)
                for v in range(5):
                    if v + 1 < 4:
                        qk(v + 1)
                    if v < 4:
                        turn(v)
                    if v >= 1:
                        pv(v - 1)
                need(pe, xo_low, 4 * hd + 4)
                for kk in range(2):
                    rows(O0 + 2 * hd + kk, kk, O_D + 2 * hd + kk, lambda half: [
                        h[:, part, bass.ds(2 * hd + kk, 1), hs(half)].rearrange("p a s -> p (a s)")
                        for part in range(2)])

            with pe.Fori(0, MEM_HEADS) as hd:
                xattn_head(hd)

            ffn(FFN2, FFN2_A, FFN2_B, FFN2_D, 3)
            need(pe, b_read, 2 * (use_b(FFN2_B) + FT))
            for half in range(2):
                for k in range(DT):
                    squares(4, half, k)

        @block.scalar
        def _(act_e):
            e = act_e
            credits(e, "act")
            e.dma_start(gn[:, :, :], gains).then_inc(const_in, 16)
            e.dma_start(mem, memT).then_inc(mem_in, 16)
            e.dma_start(tab[0:BUCKETS, :], table).then_inc(tab_in, 16)
            e.dma_start(ipos, positions).then_inc(pos_in, 16)
            e.dma_start(hot, onehot).then_inc(tab_in, 16)
            e.dma_start(x[:, :, :], xT).then_inc(x_in, 16)
            e.dma_start(cw[:, :, :], conv_w).then_inc(const_in, 16)
            e.dma_start(snk[:, :], bass.AP(sinks.tensor, 0, [[0, P], [1, HEADS]])).then_inc(const_in, 16)
            e.wait_ge(const_in, 48)
            e.wait_ge(mem_in, 16)
            for k in range(DT):
                e.activation(memh[:, 0, k, :], mem[:, k, :], ACT.Copy, scale=gn[:, 4, k:k + 1]).then_inc(m_high, 1)
                if k >= 2:
                    e.wait_ge(m_ss, k - 1)
                e.activation(sq[:, k % 2, 0:M], mem[:, k, :], ACT.Square).then_inc(m_sq, 1)
            e.wait_ge(m_ss, DT)
            e.wait_ge(vec_setup, 2)
            e.activation(rstd[:, 0:M], psD[:, 1, 0:M], ACT.Sqrt, bias=epst[:, 0:1], scale=1.0 / D).then_inc(m_root, 1)

            def bias_by_distance():
                e.wait_ge(vrow_cp, 1)
                e.dma_start(bass.AP(vrow_dram, 0, [[RUN, HEADS], [1, RUN]]), vrow).then_inc(vrow_out, 16)

            def bias_shifted():
                e.wait_ge(vrow_out, 16)
                e.dma_start(bass.AP(bias_dram, REGION, [[ROWLEN + 1, P], [1, ROWLEN]]),
                            bass.AP(vrow_dram, 0, [[0, P], [1, ROWLEN]])).then_inc(bias_made, 16)
                e.wait_ge(setup, 4)
                for q in range(4):
                    e.dma_start(region(0, 0, P, P + q * 4 * RUN, [[RUN, 4], [1, P]]),
                                negt.rearrange("p (a k) -> p a k", a=1).to_broadcast([P, 4, P])
                                ).then_inc(bias_made, 16)

            def bias_block0():
                e.wait_ge(bias_made, 16 * 5)
                e.dma_start(region(0, 0, P, 2 * P, [[RUN, HEADS], [1, P]]),
                            region(1, 0, P, 2 * P, [[RUN, HEADS], [1, P]])).then_inc(bias_made, 16)

            def tile_out(bi, half, k, gain):
                r = 16 * bi + 8 * half + k
                if gain is not None:
                    e.activation(h[:, 0, k, hs(half)], x[:, k, hs(half)], ACT.Copy,
                                 scale=gn[:, gain, k:k + 1]).then_inc(h_high, 1)
                if bi == 0:
                    need(e, ss_full, r - 1)
                e.activation(square(bi, half, k), x[:, k, hs(half)], ACT.Square).then_inc(sq_made, 1)

            def roots(bi):
                for half in range(2):
                    need(e, ss_full, 16 * bi + 8 * (half + 1))
                    e.activation(rstd[:, hs(half)], psB[:, half, :], ACT.Sqrt, bias=epst[:, 0:1],
                                 scale=1.0 / D).then_inc(root, 1)

            def boundary(bi, dn, gain):
                for half in range(2):
                    for k in range(DT):
                        if dn is not None:
                            need(e, x_added, 16 * dn + 8 * half + k + 1)
                        tile_out(bi, half, k, gain)
                roots(bi)

            e.wait_ge(x_in, 16)
            e.wait_ge(m_ss, DT)
            for half in range(2):
                for k in range(DT):
                    tile_out(0, half, k, 0)
            e.wait_ge(m_copied, 16)
            e.dma_start(kv_dram[:, 0:2, :], qkv[:, 0:2, :]).then_inc(kv_saved, 16)
            e.dma_start(kv_dram[:, 2:4, :], vnat).then_inc(kv_saved, 16)
            e.wait_ge(pos_halves, POS_STEPS)
            for c in range(2):
                e.dma_start(bass.AP(pos_dram, c * POS_ROW, [[P, 1], [1, P]]), fpad[c]).then_inc(pos_saved, 16)
                e.dma_start(bass.AP(pos_dram, c * POS_ROW + P, [[S, 1], [1, S]]), fpos[c]).then_inc(pos_saved, 16)
            bias_by_distance()
            roots(0)
            bias_shifted()

            def ffn(s0, a0, t0):
                with e.Fori(0, FT) as t:
                    for half in range(2):
                        need(e, a_read, 2 * (a0 - 4 + t) + half + 1)
                        e.activation(gate[:, hs(half)], gate[:, hs(half)], ACT.Silu).then_inc(silu_done, 1)
                    for half in range(2):
                        need(e, act_mid, 2 * (t0 + t) + half + 1)
                        e.activation(act[:, 0, hs(half)], up[:, hs(half)], ACT.Copy).then_inc(act_high, 1)

            ffn(0, FFN1_A, FFN1_T)
            bias_block0()
            e.wait_ge(kv_saved, 32)
            boundary(1, FFN1_D + FT - 1, 1)
            need(e, x_added, 16 * CONV_D)
            e.dma_start(x_dram[:, :, :], x[:, :, :]).then_inc(x_saved, 16)
            e.wait_ge(x_saved, 16)
            need(e, h_low, 32)
            e.wait_ge(tables_done, 1)

            need(e, a_read, 2 * 32)
            need(e, b_read, 2 * 32)

            def swa_block(b, par):
                blk = bass.ds(b * P, P)
                need(e, qk_done, 8 * b)
                stand(e, act_passed)
                e.activation(qs[:, 0, :, :], qkv[:, 0:DT, blk], ACT.Copy, scale=HD ** -0.5).then_inc(qs_high, 1)
                for g in range(2):
                    e.activation(kz[g * HD:(g + 1) * HD, 0, :, g, par, :], qkv[g * HD:(g + 1) * HD, 8:10, blk],
                                 ACT.Copy).then_inc(kz_high, 1)
                need(e, v_turned, b)
                stand(e, act_passed)
                e.activation(vst[:, :, :], qkv[:, 10:12, blk], ACT.Copy).then_inc(vst_made, 1)
                need(e, v_turned, b + 1)
                need(e, pv_done, 8 * b)
                e.activation(vv[:, 0, par, :], psO(1)[:, 0:256], ACT.Copy).then_inc(vv_high, 1)

                def exps(j):
                    u = 8 * b + j
                    need(e, sunk, u + 1)
                    e.activation(esk[:, j % 4, :], sk[:, j % 4, :], ACT.Exp)
                    for hh in range(2):
                        part = sc[:, j % 4, hh * 256:(hh + 1) * 256]
                        ins = e.activation(part, part, ACT.Exp, bias=nm[:, j % 4, hh:hh + 1],
                                           accum_out=rs[:, j % 4, hh:hh + 1])
                    ins.then_inc(exp_done, 1)

                def high(j):
                    u = 8 * b + j
                    need(e, turned, u + 1)
                    need(e, pv_done, u - 1)
                    e.activation(pt[:, j % 2, 0, :, :].rearrange("p s k -> p (s k)"), psT(j), ACT.Copy
                                 ).then_inc(pt_high, 1)

                def outp(j):
                    u = 8 * b + j
                    need(e, pv_done, u + 1)
                    stand(e, act_passed)
                    for hh in range(2):
                        ins = e.activation(qkv[hh * HD:(hh + 1) * HD, j, blk],
                                           psO(j)[hh * HD:(hh + 1) * HD, hh * P:(hh + 1) * P], ACT.Copy)
                    ins.then_inc(o_out, 1)

                for j in range(11):
                    if j < 8:
                        exps(j)
                    if 0 <= j - 1 < 8:
                        high(j - 1)
                    if 0 <= j - 2 < 8:
                        outp(j - 2)

            with e.Fori(0, NB // 2) as i:
                for par in range(2):
                    swa_block(2 * i + par, par)

            need(e, pv_done, 64)
            e.dma_start(x[:, :, :], x_dram[:, :, :]).then_inc(x_back, 16)

            def conv_tile(t):
                need(e, conv_v, 12 * t + 2)
                stand(e, act_passed)
                tap = cw[:, bass.ds(t, 1), 0:1].rearrange("p a b -> p (a b)")
                for half in range(2):
                    e.activation(cv[:, hs(half)], cu[:, half * HALF:(half + 1) * HALF], ACT.Copy, scale=tap
                                 ).then_inc(conv_s, 1)
                for half in range(2):
                    need(e, b_read, 2 * (CONV_B - 4 + 2 * t + 1) + half + 1)
                    e.activation(cG[:, hs(half)], cG[:, hs(half)], ACT.Sigmoid).then_inc(conv_s, 1)
                for half in range(2):
                    need(e, a_read, 2 * (CONV_A - 4 + 3 * t + 2) + half + 1)
                    e.activation(cA[:, hs(half)], cA[:, hs(half)], ACT.Sigmoid).then_inc(conv_s, 1)
                for half in range(2):
                    need(e, act_mid, 2 * (CONV_T + t) + half + 1)
                    e.activation(mrg[:, 0, hs(half)], cB[:, hs(half)], ACT.Copy).then_inc(act_high, 1)

            with e.Fori(0, DT) as t:
                conv_tile(t)
            need(e, act_low, 2 * (CONV_T + DT))
            e.dma_start(qkv[:, 8:12, :], kv_dram[:, :, :]).then_inc(kv_back, 16)
            boundary(2, CONV_D + DT - 1, 2)

            e.wait_ge(kv_back, 16)
            need(e, a_read, 2 * (FFN2_A - 4))
            need(e, b_read, 2 * (FFN2_B - 4))

            def xattn_head(hd):
                need(e, qk_done, 64 + 4 * hd)
                stand(e, act_passed)
                e.activation(kx[:, 0, :, :], kmem[:, bass.ds(2 * hd, 2), :], ACT.Copy).then_inc(kxs, 1)
                need(e, pv_done, 64 + 4 * hd)
                stand(e, act_passed)
                e.activation(vx[:, 0, :, :], vmem[:, :, bass.ds(hd * MHD, MHD)], ACT.Copy).then_inc(kxs, 1)

                def queries(v):
                    need(e, qk_done, 64 + 4 * hd + v - 1)
                    stand(e, act_passed)
                    e.activation(qx[:, v % 2, 0, :, :], qkv[:, bass.ds(2 * hd, 2), v * 256:(v + 1) * 256], ACT.Copy,
                                 scale=MHD ** -0.5).then_inc(qs_high, 1)

                def exps(v):
                    u = 64 + 4 * hd + v
                    need(e, maxed, u + 1)
                    need(e, turned, u - 1)
                    for qb in range(2):
                        part = sx[:, v % 2, qb * 256:(qb + 1) * 256]
                        ins = e.activation(part, psS(v)[:, qb * 256:(qb + 1) * 256], ACT.Exp,
                                           bias=nmx[:, v, qb:qb + 1], accum_out=rs[:, v, qb:qb + 1])
                    ins.then_inc(exp_done, 1)

                def high(v):
                    u = 64 + 4 * hd + v
                    need(e, turned, u + 1)
                    need(e, pv_done, u - 1)
                    e.activation(px[:, v % 2, 0, :, :].rearrange("p s k -> p (s k)"), psT(v), ACT.Copy
                                 ).then_inc(pt_high, 1)

                def outp(v):
                    need(e, pv_done, 64 + 4 * hd + v + 1)
                    stand(e, act_passed)
                    e.activation(h[:, 0, bass.ds(2 * hd, 2), v * 256:(v + 1) * 256],
                                 psO(v).rearrange("p (d q) -> p d q", d=2), ACT.Copy).then_inc(xo_high, 1)

                queries(0)
                queries(1)
                for v in range(6):
                    if v < 4:
                        exps(v)
                    if v + 2 < 4:
                        queries(v + 2)
                    if 0 <= v - 1 < 4:
                        high(v - 1)
                    if 0 <= v - 2 < 4:
                        outp(v - 2)

            with e.Fori(0, MEM_HEADS) as hd:
                xattn_head(hd)
            boundary(3, O_D + DT - 1, 3)
            ffn(FT, FFN2_A, FFN2_T)
            boundary(4, FFN2_D + FT - 1, None)
            for half in range(2):
                for k in range(0, DT, 4):
                    e.wait_ge(outs, 8 * half + k + 4)
                    e.dma_start(out[:, k:k + 4, hs(half)], qkv[:, k:k + 4, hs(half)]).then_inc(out_done, 16)
            e.wait_ge(out_done, 16 * 4)

        @block.vector
        def _(v_e):
            e = v_e
            credits(e, "dve")
            e.memset(tab[BUCKETS:BUCKETS + 1, :], NEG_INF).then_inc(vec_setup, 1)
            e.memset(epst[:, :], EPS).then_inc(vec_setup, 1)
            e.wait_ge(vrow_mm, 1)
            e.tensor_copy(vrow, psD[0:HEADS, 0, 0:RUN]).then_inc(vrow_cp, 1)
            e.wait_ge(const_in, 48)
            e.tensor_scalar(nsnk[:, :], snk[:, :], -1.0, None, ALU.mult).then_inc(vec_setup, 1)
            for k in range(DT):
                e.wait_ge(m_high, k + 1)
                e.scalar_tensor_tensor(out=memh[:, 1, k, :], in0=mem[:, k, :], scalar=gn[:, 4, k:k + 1],
                                       in1=memh[:, 0, k, :].bitcast(F32), op0=ALU.mult, op1=ALU.subtract
                                       ).then_inc(m_low, 1)

            steps_done = 0

            def step(ins):
                nonlocal steps_done
                steps_done += 1
                ins.then_inc(pos_halves, 1)
                e.wait_ge(pos_halves, steps_done)

            e.wait_ge(pos_in, 16)
            for b in range(NB):
                ins = e.memset(steps[:, b:b + 1], float(b - 1))
            step(ins)
            step(e.memset(fpad[0], float(POS_PAD // POS_HIGH)))
            step(e.memset(fpad[1], 0.0))
            step(e.tensor_scalar(ihalf[:, 0, :], ipos, 16, None, ALU.arith_shift_right))
            step(e.tensor_scalar(ihalf[:, 1, :], ipos, POS_HIGH - 1, None, ALU.bitwise_and))
            for c in range(2):
                step(e.tensor_copy(fpos[c], ihalf[:, c, :]))
            for c in range(2):
                step(e.tensor_tensor(fdiff[:, c, :], fpos[c][:, 1:], fpos[c][:, 0:S - 1], ALU.subtract))
            step(e.scalar_tensor_tensor(out=fdiff[:, 0, :], in0=fdiff[:, 0, :], scalar=float(POS_HIGH),
                                        in1=fdiff[:, 1, :], op0=ALU.mult, op1=ALU.add))
            step(e.tensor_scalar(fdiff[:, 0, :], fdiff[:, 0, :], 1.0, None, ALU.not_equal))
            step(e.tensor_reduce(odd[:, 0:1], fdiff[:, 0, :], AX.X, ALU.max))
            step(e.tensor_scalar(odd[:, 1:2], fpos[0][:, 0:1], float(POS_PAD // POS_HIGH - 1), None, ALU.is_ge))
            step(e.tensor_scalar(odd[:, 2:3], fpos[0][:, 0:1], float(POS_PAD // POS_HIGH), None, ALU.is_le))
            step(e.tensor_tensor(odd[:, 1:2], odd[:, 1:2], odd[:, 2:3], ALU.mult))
            step(e.tensor_tensor(odd[:, 0:1], odd[:, 0:1], odd[:, 1:2], ALU.max))
            step(e.tensor_copy(flags[:, 0:1], odd[:, 0:1]))
            step(e.tensor_scalar(flags[:, 1:], steps[:, :], odd[:, 0:1], 1.0, ALU.mult, ALU.add))

            e.wait_ge(m_root, 1)
            e.reciprocal(rstd[:, 0:M], rstd[:, 0:M]).then_inc(m_rstd, 1)
            e.wait_ge(m_rstd, 1)
            with e.Fori(0, KV_BLOCKS // 2) as i:
                for par, (bank, read) in enumerate(((psA, a_read), (psB, b_read))):
                    need(e, half_done, 2 * (2 * i + par) + 2)
                    e.tensor_tensor(kvT[:, bass.ds(2 * i + par, 1), :].rearrange("p a m -> p (a m)"),
                                    bank[:, 0, 0:M], rstd[:, 0:M], ALU.mult).then_inc(read, 1)
            for t in range(DT):
                for mt in range(2):
                    n = 2 * t + mt
                    e.wait_ge(m_turned, n + 1)
                    e.tensor_copy(vnat[:, mt, t * P:(t + 1) * P], psD[:, 2 + n % 2, 0:P]).then_inc(m_copied, 1)

            def low(bi, half, k, gain):
                r = 16 * bi + 8 * half + k
                need(e, h_high, r + 1)
                e.scalar_tensor_tensor(out=h[:, 1, k, hs(half)], in0=x[:, k, hs(half)], scalar=gn[:, gain, k:k + 1],
                                       in1=h[:, 0, k, hs(half)].bitcast(F32), op0=ALU.mult, op1=ALU.subtract
                                       ).then_inc(h_low, 1)

            def rstds(bi):
                for half in range(2):
                    need(e, root, 2 * bi + half + 1)
                    e.reciprocal(rstd[:, hs(half)], rstd[:, hs(half)]).then_inc(rstd_made, 1)
                need(e, rstd_made, 2 * bi + 2)

            def add(n, dn, r, scale):
                half, m = r // 8, r % 8
                if m == 7:
                    need(e, half_done, 2 * n + half + 1)
                else:
                    need(e, d_full, 14 * dn + 7 * half + m + 1)
                need(e, x_added, 16 * dn + r - 15)
                e.scalar_tensor_tensor(out=x[:, m, hs(half)], in0=psD[:, r % 4, :], scalar=scale,
                                       in1=x[:, m, hs(half)], op0=ALU.mult, op1=ALU.add).then_inc(x_added, 1)

            def boundary(bi, n, dn, scale, gain):
                for r in range(17):
                    if r < 16:
                        add(n, dn, r, scale)
                    if r >= 1 and gain is not None:
                        low(bi, (r - 1) // 8, (r - 1) % 8, gain)
                rstds(bi)

            e.wait_ge(x_in, 16)
            for half in range(2):
                for k in range(DT):
                    low(0, half, k, 0)
            rstds(0)

            def ffn(n0, s0, t0, dn0):
                b1 = 2 * ((FFN1_B if n0 == FFN1 else FFN2_B) - 4)
                def gates(t):
                    n = n0 + 3 * t - 1 if not isinstance(t, int) else n0
                    for half in range(2):
                        need(e, half_done, 2 * n + half + 1)
                        e.tensor_tensor(gate[:, hs(half)], psA[:, half, :], rstd[:, hs(half)], ALU.mult
                                        ).then_inc(a_read, 1)

                def ups(t):
                    for half in range(2):
                        need(e, half_done, 2 * (n0 + 3 * t + 1) + half + 1)
                        e.tensor_tensor(up[:, hs(half)], psB[:, half, :], rstd[:, hs(half)], ALU.mult
                                        ).then_inc(b_read, 1)
                        need(e, b_read, b1 + 2 * t + half + 1)
                        need(e, silu_done, 2 * (s0 + t) + half + 1)
                        e.tensor_tensor(up[:, hs(half)], up[:, hs(half)], gate[:, hs(half)], ALU.mult
                                        ).then_inc(act_mid, 1)
                    for half in range(2):
                        need(e, act_high, 2 * (t0 + t) + half + 1)
                        need(e, act_mid, 2 * (t0 + t) + half + 1)
                        e.tensor_tensor(act[:, 1, hs(half)], up[:, hs(half)], act[:, 0, hs(half)].bitcast(F32),
                                        ALU.subtract).then_inc(act_low, 1)

                gates(0)
                ups(0)
                with e.Fori(1, FT) as t:
                    gates(t)
                    for r in range(16):
                        add(n0 + 3 * t, dn0 + t - 1, r, 0.5)
                    ups(t)

            ffn(FFN1, 0, FFN1_T, FFN1_D)
            boundary(1, QKV0 - 1, FFN1_D + FT - 1, 0.5, 1)

            def project(i, n0):
                for par, (bank, read) in enumerate(((psA, a_read), (psB, b_read))):
                    for half in range(2):
                        need(e, half_done, 2 * (n0 + 2 * i + par) + half + 1)
                        e.tensor_tensor(qkv[:, bass.ds(2 * i + par, 1), hs(half)].rearrange("p a s -> p (a s)"),
                                        bank[:, half, :], rstd[:, hs(half)], ALU.mult).then_inc(read, 1)

            e.wait_ge(kv_saved, 32)
            e.wait_ge(bias_made, 16 * 6)
            with e.Fori(0, QKV_BLOCKS // 2) as i:
                project(i, QKV0)

            need(e, a_read, 2 * 32)
            need(e, b_read, 2 * 32)
            e.wait_ge(x_saved, 16)
            e.wait_ge(tables_done, 1)
            for g in range(2):
                e.memset(kz[g * HD:(g + 1) * HD, :, :, 1 - g, :, :].bitcast(F32), 0.0).then_inc(vec_setup, 1)
                e.memset(kz[g * HD:(g + 1) * HD, :, :, g, 1, :].bitcast(F32), 0.0).then_inc(vec_setup, 1)
            e.memset(vv[:, :, 1, :].bitcast(F32), 0.0).then_inc(vec_setup, 1)
            e.wait_ge(vec_setup, 8)

            def swa_block(b, par):
                blk = bass.ds(b * P, P)
                need(e, qs_high, b + 1)
                e.scalar_tensor_tensor(out=qs[:, 1, :, :], in0=qkv[:, 0:DT, blk], scalar=HD ** -0.5,
                                       in1=qs[:, 0, :, :].bitcast(F32), op0=ALU.mult, op1=ALU.subtract
                                       ).then_inc(qs_low, 1)
                for g in range(2):
                    need(e, kz_high, 2 * b + g + 1)
                    rows_g = slice(g * HD, (g + 1) * HD)
                    e.tensor_tensor(kz[rows_g, 1, :, g, par, :], qkv[rows_g, 8:10, blk],
                                    kz[rows_g, 0, :, g, par, :].bitcast(F32), ALU.subtract).then_inc(kz_low, 1)
                need(e, vv_high, b + 1)
                e.tensor_tensor(vv[:, 1, par, :], psO(1)[:, 0:256], vv[:, 0, par, :].bitcast(F32), ALU.subtract
                                ).then_inc(vv_low, 1)

                def score(j):
                    u = 8 * b + j
                    need(e, qk_done, u + 1)
                    e.wait_ge(bias_in[j % 4], 32 * (2 * b + j // 4 + 1))
                    need(e, turned, u - 3)
                    ring = j % 4
                    e.tensor_tensor(sc[:, ring, :], psS(j), bias[:, ring, :], ALU.add).then_inc(scored, 1)
                    need(e, scored, u + 1)
                    e.tensor_reduce(nmx[:, ring, :], sc[:, ring, :].rearrange("p (h k) -> p h k", h=2), AX.X, ALU.max,
                                    negate=True).then_inc(maxed, 1)
                    need(e, maxed, u + 1)
                    e.tensor_tensor(nm[:, ring, :], nmx[:, ring, :], nsnk[:, 2 * j:2 * j + 2], ALU.min
                                    ).then_inc(shifted, 1)
                    need(e, shifted, u + 1)
                    e.tensor_tensor(sk[:, ring, :], nm[:, ring, :], snk[:, 2 * j:2 * j + 2], ALU.add
                                    ).then_inc(sunk, 1)

                def invert(j):
                    u = 8 * b + j
                    ring = j % 4
                    need(e, exp_done, u + 1)
                    e.tensor_tensor(den[:, ring, :], rs[:, ring, :], esk[:, ring, :], ALU.add).then_inc(summed, 1)
                    need(e, summed, u + 1)
                    e.reciprocal(rden[:, ring, :], den[:, ring, :]).then_inc(inverted, 1)

                def low_part(j):
                    need(e, pt_high, 8 * b + j + 1)
                    e.tensor_tensor(pt[:, j % 2, 1, :, :].rearrange("p s k -> p (s k)"), psT(j),
                                    pt[:, j % 2, 0, :, :].rearrange("p s k -> p (s k)").bitcast(F32), ALU.subtract
                                    ).then_inc(pt_low, 1)

                for j in range(10):
                    if j < 8:
                        score(j)
                    if 0 <= j - 1 < 8:
                        invert(j - 1)
                    if 0 <= j - 2 < 8:
                        low_part(j - 2)

            with e.Fori(0, NB // 2) as i:
                for par in range(2):
                    swa_block(2 * i + par, par)

            e.memset(cu[:, 0:2], 0.0).then_inc(vec_setup, 1)
            e.wait_ge(vec_setup, 9)
            need(e, o_out, 64)
            a0, b0 = CONV_A - 4, CONV_B - 4

            def conv_tile(t, peeled):
                v = 12 * t
                A, B = a0 + 3 * t, b0 + 2 * t

                n = CONV0 if peeled else CONV0 - 1 + 6 * t
                k = 2 if peeled else 3

                def scaled(dst, bank, read, n):
                    for half in range(2):
                        need(e, half_done, 2 * n + half + 1)
                        e.tensor_tensor(dst[:, hs(half)], bank[:, half, :], rstd[:, hs(half)], ALU.mult
                                        ).then_inc(read, 1)

                scaled(cC, psA, a_read, n)
                scaled(cu[:, 2:], psB, b_read, n + 1)
                need(e, a_read, 2 * A + 2)
                for half in range(2):
                    need(e, b_read, 2 * B + half + 1)
                    seg = cu[:, 2 + half * HALF:2 + (half + 1) * HALF]
                    e.tensor_tensor(seg, seg, cC[:, hs(half)], ALU.mult).then_inc(conv_v, 1)
                if not peeled:
                    for r in range(16):
                        add(n + 2, CONV_D + t - 1, r, 1.0)
                cwt = cw[:, t:t + 1, :] if isinstance(t, int) else cw[:, bass.ds(t, 1), :]
                for tap in (1, 2):
                    for half in range(2):
                        if tap == 1:
                            need(e, conv_s, 6 * t + half + 1)
                            need(e, conv_v, v + 2)
                        else:
                            need(e, conv_v, v + 2 + half + 1)
                        e.scalar_tensor_tensor(out=cv[:, hs(half)], in0=cu[:, tap + half * HALF:tap + (half + 1) * HALF],
                                               scalar=cwt[:, :, tap:tap + 1].rearrange("p a b -> p (a b)"),
                                               in1=cv[:, hs(half)], op0=ALU.mult, op1=ALU.add).then_inc(conv_v, 1)
                scaled(cB, psA, a_read, n + k)
                need(e, a_read, 2 * (A + 1) + 2)
                for half in range(2):
                    need(e, conv_v, v + 4 + half + 1)
                    e.tensor_tensor(cB[:, hs(half)], cB[:, hs(half)], cv[:, hs(half)], ALU.mult).then_inc(conv_v, 1)
                scaled(cG, psB, b_read, n + k + 1)
                for half in range(2):
                    need(e, conv_s, 6 * t + 2 + half + 1)
                    need(e, conv_v, v + 6 + half + 1)
                    e.tensor_tensor(cB[:, hs(half)], cB[:, hs(half)], cG[:, hs(half)], ALU.mult).then_inc(conv_v, 1)
                scaled(cA, psA, a_read, n + k + 2)
                att = qkv[:, t, :] if isinstance(t, int) else qkv[:, bass.ds(t, 1), :].rearrange("p a s -> p (a s)")
                for half in range(2):
                    need(e, conv_s, 6 * t + 4 + half + 1)
                    e.tensor_tensor(cA[:, hs(half)], cA[:, hs(half)], att[:, hs(half)], ALU.mult).then_inc(conv_v, 1)
                for half in range(2):
                    need(e, conv_v, v + 10 + half + 1)
                    e.tensor_tensor(cB[:, hs(half)], cB[:, hs(half)], cA[:, hs(half)], ALU.add).then_inc(act_mid, 1)
                for half in range(2):
                    n = 2 * (CONV_T + t) + half + 1
                    need(e, act_high, n)
                    need(e, act_mid, n)
                    e.tensor_tensor(mrg[:, 1, hs(half)], cB[:, hs(half)], mrg[:, 0, hs(half)].bitcast(F32),
                                    ALU.subtract).then_inc(act_low, 1)

            conv_tile(0, True)
            e.wait_ge(x_back, 16)
            with e.Fori(1, DT) as t:
                conv_tile(t, False)
            boundary(2, Q0 - 1, CONV_D + DT - 1, 1.0, 2)

            with e.Fori(0, Q_BLOCKS // 2) as i:
                project(i, Q0)
            e.wait_ge(kv_back, 16)

            def xattn_head(hd, last):
                need(e, kxs, 2 * hd + 1)
                e.tensor_tensor(kx[:, 1, :, :], kmem[:, bass.ds(2 * hd, 2), :], kx[:, 0, :, :].bitcast(F32),
                                ALU.subtract).then_inc(kxl, 1)
                need(e, kxs, 2 * hd + 2)
                e.tensor_tensor(vx[:, 1, :, :], vmem[:, :, bass.ds(hd * MHD, MHD)], vx[:, 0, :, :].bitcast(F32),
                                ALU.subtract).then_inc(kxl, 1)

                def queries(v):
                    need(e, qs_high, NB + 4 * hd + v + 1)
                    e.scalar_tensor_tensor(out=qx[:, v % 2, 1, :, :],
                                           in0=qkv[:, bass.ds(2 * hd, 2), v * 256:(v + 1) * 256],
                                           scalar=MHD ** -0.5, in1=qx[:, v % 2, 0, :, :].bitcast(F32),
                                           op0=ALU.mult, op1=ALU.subtract).then_inc(qs_low, 1)

                def maxes(v):
                    u = 64 + 4 * hd + v
                    need(e, qk_done, u + 1)
                    e.tensor_reduce(nmx[:, v, :], psS(v).rearrange("p (h k) -> p h k", h=2), AX.X, ALU.max,
                                    negate=True).then_inc(maxed, 1)

                def invert(v):
                    u = 64 + 4 * hd + v
                    need(e, exp_done, u + 1)
                    e.reciprocal(rden[:, v, :], rs[:, v, :]).then_inc(inverted, 1)
                    e.sem_inc(scored, 1)

                def low_part(v):
                    need(e, pt_high, 64 + 4 * hd + v + 1)
                    e.tensor_tensor(px[:, v % 2, 1, :, :].rearrange("p s k -> p (s k)"), psT(v),
                                    px[:, v % 2, 0, :, :].rearrange("p s k -> p (s k)").bitcast(F32), ALU.subtract
                                    ).then_inc(pt_low, 1)

                def outp(v):
                    need(e, xo_high, 4 * hd + v + 1)
                    dst = h[:, :, bass.ds(2 * hd, 2), v * 256:(v + 1) * 256]
                    e.tensor_tensor(dst[:, 1, :, :], psO(v).rearrange("p (d q) -> p d q", d=2),
                                    dst[:, 0, :, :].bitcast(F32), ALU.subtract).then_inc(xo_low, 1)

                queries(0)
                queries(1)
                for v in range(6):
                    if v < 4:
                        maxes(v)
                    if 0 <= v - 1 < 4:
                        invert(v - 1)
                    if 2 <= v + 1 < 4:
                        queries(v + 1)
                    if 0 <= v - 1 < 4:
                        low_part(v - 1)
                    if 0 <= v - 2 < 4:
                        outp(v - 2)
                for kk in range(2 - last):
                    for r in range(16):
                        add(O0 + 2 * hd + kk, O_D + 2 * hd + kk, r, 1.0)

            with e.Fori(0, MEM_HEADS - 1) as hd:
                xattn_head(hd, 0)
            xattn_head(MEM_HEADS - 1, 1)
            boundary(3, FFN2 - 1, O_D + DT - 1, 1.0, 3)

            ffn(FFN2, FT, FFN2_T, FFN2_D)
            boundary(4, BLOCKS - 1, FFN2_D + FT - 1, 0.5, None)
            for half in range(2):
                for k in range(DT):
                    e.scalar_tensor_tensor(out=qkv[:, k, hs(half)], in0=x[:, k, hs(half)],
                                           scalar=gn[:, 5, k:k + 1], in1=rstd[:, hs(half)],
                                           op0=ALU.mult, op1=ALU.mult).then_inc(outs, 1)


def launch_arrays(x, mem, positions, rel_bias, ffn1_norm, ffn1_w_gu, ffn1_w_down, mix_norm, w_in, sinks, conv_w,
                  w_out, xattn_norm, mem_norm, xattn_wq, xattn_wkv, xattn_wo, ffn2_norm, ffn2_w_gu, ffn2_w_down,
                  final_norm):
    group = HEADS // KVH
    order = [2 * (j // group) * group + half * group + j % group for j in range(DT) for half in range(2)]
    chan = np.concatenate([np.arange(o * HD, (o + 1) * HD) for o in order])

    def tiles(a):
        return a.reshape(-1, P, a.shape[1]).transpose(1, 0, 2)

    def columns(w):
        return w.reshape(DT, P, -1, P).transpose(2, 1, 0, 3).reshape(-1, P, D)

    def rows(w):
        return w.reshape(-1, P, D)

    def ffn(gu, down):
        gate, up, dn = columns(gu[:, :F]), columns(gu[:, F:]), rows(down)
        seq = [gate[0:1], up[0:1]]
        for t in range(1, FT):
            seq += [gate[t:t + 1], dn[t - 1:t], up[t:t + 1]]
        return seq + [dn[FT - 1:FT]]

    w = w_in[0]
    at = np.cumsum([0, D, KVH * HD, KVH * HD, D, D, D, D, D])
    q, k, v, c, b, u, ga, gc = (w[:, at[n]:at[n + 1]] for n in range(8))
    c, b, u, ga, gc = (columns(m[:, chan]) for m in (c, b, u, ga, gc))
    wo = rows(w_out[0][chan, :])
    blocks = [columns(xattn_wkv[0])]
    blocks += ffn(ffn1_w_gu[0], ffn1_w_down[0])
    blocks += [columns(q[:, chan]), columns(k), columns(v)]
    for t in range(DT):
        one = slice(t, t + 1)
        blocks += [c[one], u[one]] + ([wo[t - 1:t]] if t else []) + [b[one], gc[one], ga[one]]
    blocks += [wo[DT - 1:DT], columns(xattn_wq[0]), rows(xattn_wo[0])]
    blocks += ffn(ffn2_w_gu[0], ffn2_w_down[0])

    onehot = np.zeros((BUCKETS + 1, RUN), np.float32)
    for m in range(RUN):
        rel = 2 * P - m
        onehot[bucket(rel) if 0 <= rel < WINDOW else BUCKETS, m] = 1.0

    gains = np.stack([g.reshape(DT, P).T for g in
                      (ffn1_norm[0], mix_norm[0], xattn_norm[0], ffn2_norm[0], mem_norm[0], final_norm)], 1)
    return {
        "xT": tiles(x[0].T), "memT": tiles(mem[0].T), "weights": np.concatenate(blocks, 0), "gains": gains,
        "conv_w": conv_w[0][:, chan].reshape(3, DT, P).transpose(2, 1, 0), "table": rel_bias[:, order],
        "onehot": onehot, "sinks": sinks[:, order], "positions": positions,
    }


def bucket(n):
    return int(np.searchsorted(STARTS, n, side="right")) - 1


STARTS = list(range(16)) + [int(np.ceil(16 * (MAX_DIST / 16) ** (n / 16) - 1e-9)) for n in range(16)]


def kernel(**inputs):
    import concourse.bacc as bacc
    from concourse.bass_utils import run_bass_kernel_spmd

    nc = bacc.Bacc("TRN2", target_bir_lowering=False, num_devices=1)
    arrays, args = {}, {}
    for name, a in launch_arrays(**{k: np.asarray(v) for k, v in inputs.items()}).items():
        a = np.ascontiguousarray(a)
        arrays[f"in_{name}"] = a
        args[name] = nc.dram_tensor(f"in_{name}", a.shape, mybir.dt.from_np(a.dtype), kind="ExternalInput").ap()
    out = nc.dram_tensor("out_T", (P, DT, S), F32, kind="ExternalOutput").ap()
    build(nc, *[args[n] for n in ("xT", "memT", "weights", "gains", "conv_w", "table", "onehot", "sinks",
                                  "positions")], out)
    got = run_bass_kernel_spmd(nc, [arrays], core_ids=[0]).results[0]["out_T"]
    return np.asarray(got).transpose(1, 0, 2).reshape(D, S).T[None]
```

```python
from contextlib import ExitStack

import numpy as np

import concourse.bass as bass
from concourse import mybir

F32, F32R, I32 = mybir.dt.float32, mybir.dt.float32r, mybir.dt.int32
ALU, ACT, AX = mybir.AluOpType, mybir.ActivationFunctionType, mybir.AxisListType

P = 128
D, S, F, M = 1024, 1024, 2816, 256
HALF = 512
DT, FT, NB = D // P, F // P, S // P
HEADS, KVH, HD = 16, 4, 64
MEM_HEADS, MHD = 4, 256
BUCKETS, MAX_DIST, WINDOW = 32, 128, 128
EPS, NEG_INF = 1e-6, -1e30

RUN = 384
ROWLEN = HEADS * RUN
REGION = P * ROWLEN + P * 3
POS_PAD = 1 << 30
POS_HIGH = 1 << 16
POS_ROW = P + S

KV_BLOCKS, FFN_BLOCKS, QKV_BLOCKS, CONV_BLOCKS, Q_BLOCKS, O_BLOCKS = 16, 3 * FT, 12, 48, 8, 8
KV0 = 0
FFN1 = KV0 + KV_BLOCKS
QKV0 = FFN1 + FFN_BLOCKS
CONV0 = QKV0 + QKV_BLOCKS
Q0 = CONV0 + CONV_BLOCKS
O0 = Q0 + Q_BLOCKS
FFN2 = O0 + O_BLOCKS
BLOCKS = FFN2 + FFN_BLOCKS

FFN1_D, CONV_D, O_D, FFN2_D = 0, FT, FT + DT, FT + 2 * DT
FFN1_T, CONV_T, FFN2_T = 0, FT, FT + DT
FFN1_A = FFN1_B = KV_BLOCKS // 2
QKV_A = QKV_B = FFN1_A + FT
CONV_A = CONV_B = QKV_A + QKV_BLOCKS // 2
Q_A, Q_B = CONV_A + 3 * DT, CONV_B + 2 * DT
FFN2_A, FFN2_B = Q_A + Q_BLOCKS // 2, Q_B + Q_BLOCKS // 2
UNITS = NB * DT

CREDIT = 32

POOL_OUT = ((4, 5, 6, 7), (6, 7))
LAG = 4
POS_STEPS = 18


def need(eng, sem, n):
    if isinstance(n, int) and n <= 0:
        return
    eng.wait_ge(sem, n + CREDIT)


def stand(eng, passed):
    eng.sem_inc(passed, 1)


def hs(h):
    return slice(h * HALF, (h + 1) * HALF)


def build(nc, xT, memT, weights, gains, conv_w, table, onehot, sinks, positions, out):
    with ExitStack() as ctx:
        def sb(name, shape, dt=F32):
            return ctx.enter_context(nc.sbuf_tensor(name, shape, dt))

        def psum(name, shape):
            return ctx.enter_context(nc.psum_tensor(name, shape, F32))

        def sem(name):
            return ctx.enter_context(nc.semaphore(name))

        def overlay(*groups):
            found, biggest = [], max(groups, key=lambda g: sum(int(np.prod(s[1:])) for _, s, _ in g))
            for g in groups:
                if g is not biggest:
                    with ExitStack() as inner:
                        found += [inner.enter_context(nc.sbuf_tensor(*t)) for t in g]
            found += [ctx.enter_context(nc.sbuf_tensor(*t)) for t in biggest]
            byname = {t.name: t for t in found}
            return [byname[n] for g in groups for n, _, _ in g]

        h = sb("h", [P, 2, DT, S], F32R)
        x, kz, vv, qs, pt = overlay(
            [("x", [P, DT, S], F32)],
            [("kz", [P, 2, 2, 2, 2, P], F32R),
             ("vv", [P, 2, 2, 256], F32R),
             ("qs", [P, 2, DT, P], F32R),
             ("pt", [P, 2, 2, 2, 256], F32R)])
        qkv = sb("qkv", [P, QKV_BLOCKS, S])
        wsp = sb("wsp", [P, 2, 2, 1024], F32R)
        raw = sb("raw", [P, 2, 1024])
        rstd, kx1 = overlay([("rstd", [P, S], F32)],
                            [("kx1", [P, 2, 2, M], F32R)])
        sq, vx1 = overlay([("sq", [P, 2, HALF], F32)],
                          [("vx1", [P, 2, 2, MHD], F32R)])
        memh, act, gate, up, bias, sc, vst, mrg, cu, cv, kx0, vx0, qx, sx, px = overlay(
            [("memh", [P, 2, DT, M], F32R)],
            [("act", [P, 2, S], F32R), ("gate", [P, S], F32), ("up", [P, S], F32)],
            [("bias", [P, 4, HALF], F32),
             ("sc", [P, 4, 2, 258], F32),
             ("vst", [P, 2, P], F32)],
            [("mrg", [P, 2, S], F32R), ("cu", [P, S + 2], F32), ("cv", [P, S], F32)],
            [("kx0", [P, 2, 2, M], F32R), ("vx0", [P, 2, 2, MHD], F32R), ("qx", [P, 2, 2, 2, 256], F32R),
             ("sx", [P, 2, HALF], F32), ("px", [P, 2, 2, 2, 256], F32R)])
        kx, vx = (kx0, kx1), (vx0, vx1)
        gn = sb("gn", [P, 6, DT])
        cw = sb("cw", [P, DT, 3])
        ident = sb("ident", [P, P])
        mean = sb("mean", [P, P])
        epst = sb("epst", [P, 1])
        warmed = sb("warmed", [P, 2])
        snk = sb("snk", [P, HEADS])
        tab = sb("tab", [BUCKETS + 1, HEADS])
        nmx = sb("nmx", [P, 4, 2])
        rs = sb("rs", [P, 4, 2])
        rden = sb("rden", [P, 4, 2])
        hot = qkv[0:BUCKETS + 1, 6, 0:RUN]
        vrow = qkv[0:HEADS, 7, 0:RUN]
        negt = qkv[:, 8, 0:P]
        ipos = qkv[0:1, 11, :].bitcast(I32)
        work = (qkv[0:1, 4, :], qkv[0:1, 5, :])
        fpos = (qkv[0:1, 6, :], qkv[0:1, 7, :])
        fpad = (qkv[0:1, 8, P:2 * P], qkv[0:1, 8, 2 * P:3 * P])
        odd = sb("odd", [1, 4])
        steps = sb("steps", [1, NB])
        flags = sb("flags", [1, 1 + NB], I32)
        mem = qkv[:, 4:6, :].rearrange("p a (b m) -> p (a b) m", m=M)
        kvT = qkv[:, 0:4, :].rearrange("p a (b m) -> p (a b) m", m=M)
        vnat = qkv[:, 9:11, :]
        kmem = qkv[:, 8:10, :].rearrange("p a (b m) -> p (a b) m", m=M)
        vmem = qkv[:, 10:12, :]
        cC, cB, cG, cA = (qkv[:, 8 + n, :] for n in range(4))

        acc = x[:, 0:4, :].rearrange("p a (b k) -> p (a b) k", k=2 * P)
        prod = x[:, 4:8, :].rearrange("p a (b k) -> p (a b) k", k=2 * P)
        krow = bias[:, 0, :].rearrange("p (c k) -> p c k", c=2)
        rel, hit = bias[:, 1, 0:2 * P], bias[:, 1, 2 * P:4 * P]
        bkt, one_of = bias[:, 2, 0:2 * P], bias[:, 2, 2 * P:4 * P]
        qcol = bias[:, 3, 0:2]
        trow = sc[:, 0:2, :, :].rearrange("p a h k -> p (a h k)")

        def square(bi, half, k):
            return sq[:, k % 2, :] if bi == 0 else qkv[:, k, hs(half)]

        psA = psum("psA", [P, 2, HALF])
        psB = psum("psB", [P, 2, HALF])
        psD = psum("psD", [P, 4, HALF])

        def psS(n):
            return psA[:, n % 4, :] if n % 4 < 2 else psB[:, n % 4 - 2, :]

        def psQ(n):
            return psA[:, n % 2, :] if n % 4 != 2 else psB[:, 0, :]

        psV = psB[:, 1, 0:P]

        def psT(n):
            return psD[:, n % 2, :]

        def psO(n):
            return psD[:, 2 + n % 2, :]

        bias_dram = nc.dram_tensor("bias_dram", (NB * REGION,), F32)
        vrow_dram = nc.dram_tensor("vrow_dram", (ROWLEN,), F32)
        kv_dram = nc.dram_tensor("kv_dram", (P, 4, 1024), F32)
        x_dram = nc.dram_tensor("x_dram", (P, DT, S), F32)
        pos_dram = nc.dram_tensor("pos_dram", (2 * POS_ROW,), F32)

        const_in = sem("const_in")
        gains_in = sem("gains_in")
        mem_in = [sem("mem_in0"), sem("mem_in1")]
        x_in = [sem("x_in0"), sem("x_in1")]
        out_done = sem("out_done")
        tab_in = sem("tab_in")
        vrow_out = sem("vrow_out")
        bias_made = sem("bias_made")
        pos_in = sem("pos_in")
        pos_halves = sem("pos_halves")
        pos_saved = sem("pos_saved")
        rows_in = sem("rows_in")
        region_out = sem("region_out")
        gen = sem("gen")
        tables_done = sem("tables_done")
        kv_saved, kv_back = sem("kv_saved"), sem("kv_back")
        x_saved, x_back = sem("x_saved"), sem("x_back")
        raw_in = [sem("raw_in0"), sem("raw_in1")]
        bias_in = [sem(f"bias_in{n}") for n in range(4)]
        setup = sem("setup")
        vec_setup = sem("vec_setup")
        vrow_mm = sem("vrow_mm")
        vrow_cp = sem("vrow_cp")

        counted = {}

        def csem(name, engine):
            s = sem(name)
            counted.setdefault(engine, []).append(s)
            return s

        w_high = csem("w_high", "pool")
        w_ready = csem("w_ready", "pool")
        half_done = csem("half_done", "pe")
        d_full = csem("d_full", "pe")
        ss_full = csem("ss_full", "pe")
        a_read, b_read = csem("a_read", "dve"), csem("b_read", "dve")
        x_added = csem("x_added", "dve")
        h_high = csem("h_high", "act")
        h_low = csem("h_low", "dve")
        sq_made = csem("sq_made", "act")
        root = csem("root", "act")
        sq_summed = csem("sq_summed", "pool")
        rstd_made = csem("rstd_made", "dve")
        silu_done = csem("silu_done", "act")
        act_mid = csem("act_mid", "dve")
        act_high = csem("act_high", "act")
        act_low = csem("act_low", "dve")
        qs_high, qs_low = csem("qs_high", "act"), csem("qs_low", "pool")
        xq_high, xq_low = csem("xq_high", "act"), csem("xq_low", "pool")
        kz_high, kz_low = csem("kz_high", "act"), csem("kz_low", "dve")
        vst_made = csem("vst_made", "act")
        v_turned = csem("v_turned", "pe")
        vv_high, vv_low = csem("vv_high", "act"), csem("vv_low", "dve")
        qk_done = csem("qk_done", "pe")
        scored = csem("scored", "dve")
        sunk = csem("sunk", "dve")
        maxed = csem("maxed", "dve")
        exp_done = csem("exp_done", "act")
        inverted = csem("inverted", "dve")
        normed = csem("normed", "pool")
        turned = csem("turned", "pe")
        pt_high, pt_low = csem("pt_high", "act"), csem("pt_low", "dve")
        pv_done = csem("pv_done", "pe")
        o_out = csem("o_out", "act")
        conv_v = csem("conv_v", "dve")
        conv_s = csem("conv_s", "act")
        xo_high, xo_low = csem("xo_high", "act"), csem("xo_low", "dve")
        act_passed, pool_passed = sem("act_passed"), sem("pool_passed")
        m_high, m_low = sem("m_high"), sem("m_low")
        m_sq, m_ss, m_root, m_rstd = sem("m_sq"), sem("m_ss"), sem("m_root"), sem("m_rstd")
        m_turned, m_copied = sem("m_turned"), sem("m_copied")
        outs, outs_pool = sem("outs"), sem("outs_pool")
        out_scaled = [sem("out_scaled0"), sem("out_scaled1")]
        kxs, kxl = csem("kxs", "act"), csem("kxl", "dve")

        def credits(eng, name):
            for s in counted[name]:
                eng.sem_inc(s, CREDIT)

        def region(r, q0, nq, extra, dims):
            return bass.AP(bias_dram, r * REGION + q0 * ROWLEN + extra, [[ROWLEN, nq], *dims])

        def windows(eng, slot):
            for t in range(-4, 12):
                slot(0, t)
            with eng.Fori(1, NB // 2) as i:
                for t in range(-4, 12):
                    slot(i, t)
            for t in range(12, 12 + 4 + LAG):
                slot(NB // 2 - 1, t)

        def unit(i, t):
            if isinstance(i, int) and not 0 <= 16 * i + t < NB * DT:
                return None
            return 16 * i + t, 2 * i + t // 8, t // 8 % 2, t % 8

        def prepared(i, t, at):
            if t % 4 != at or t >= 12 or (isinstance(i, int) and 16 * i + t < -4):
                return None
            g = t // 4 + 1
            return 4 * i + g, 2 * i + g // 2, g // 2 % 2, g % 2

        def added(bi, half):
            return range(DT // 2, DT) if (bi, half) == (4, 1) else range(DT)

        def sums(bi, half):
            return 2 * (DT - 1) * (bi - 1) + (DT - 1) * half + len(added(bi, half)) - 1

        def ss_event(bi, half):
            return DT * (half + 1) if bi == 0 else 2 * DT + 2 * (bi - 1) + half + 1

        def xq(w):
            return qkv[:, 2 * (w // 4):2 * (w // 4) + 2, w % 4 * 256:(w % 4 + 1) * 256]

        block = ctx.enter_context(nc.Block())

        @block.sync
        def _(sp):
            def fetch(n, s):
                sp.dma_start(raw[:, s, :], weights[n, :, :] if isinstance(n, int)
                             else weights[bass.ds(n, 1), :, :].rearrange("a p n -> p (a n)")).then_inc(raw_in[s], 16)

            for part in range(2):
                sp.dma_start(mem[:, 4 * part:4 * part + 4, :], memT[:, 4 * part:4 * part + 4, :]
                             ).then_inc(mem_in[part], 16)
            fetch(0, 0)
            fetch(1, 1)
            with sp.Fori(1, CONV0 // 2 + 1) as i:
                for s in range(2):
                    need(sp, w_ready, 2 * i + s - 1)
                    fetch(2 * i + s, s)

            sp.wait_ge(tables_done, 1)

            def bias_unit(r, par, j, u):
                need(sp, scored, u - 3)
                dst = bias[:, j % 4, :].rearrange("p (h s k) -> p h s k", h=2, s=2)
                if par:
                    sp.dma_start(bias[:, j % 4, :].rearrange("p (h k) -> p h k", h=2),
                                 region(r, 0, P, 2 * j * RUN + P, [[RUN, 2], [1, 2 * P]])).then_inc(bias_in[j % 4], 16)
                    return
                for half in range(2):
                    sp.dma_start(dst[:, :, 1 - half, :], region(r, 0, P, 2 * j * RUN + P + half * P, [[RUN, 2], [1, P]])
                                 ).then_inc(bias_in[j % 4], 16)

            for j in range(8):
                bias_unit(0, 0, j, j)
            for j in range(8):
                bias_unit(1, 1, j, 8 + j)
            with sp.Fori(1, NB // 2) as i:
                for par in range(2):
                    r = sp.value_load(flags[0:1, bass.ds(1 + 2 * i + par, 1)], min_val=1, max_val=NB - 1)
                    for j in range(8):
                        bias_unit(r, par, j, 16 * i + 8 * par + j)

            with sp.Fori(CONV0 // 2 + 1, BLOCKS // 2) as i:
                for s in range(2):
                    need(sp, w_ready, 2 * i + s - 1)
                    fetch(2 * i + s, s)

        @block.gpsimd
        def _(pool):
            credits(pool, "pool")
            pool.memset(ident[:, :], 0.0).then_inc(setup, 1)
            pool.memset(mean[:, :], 1.0 / D).then_inc(setup, 1)
            pool.memset(negt, NEG_INF).then_inc(setup, 1)
            pool.wait_ge(setup, 3)
            pool.affine_select(out=ident[:, :], in_=ident[:, :], compare_op=ALU.not_equal, fill=1.0,
                               base=0, pattern=[[-1, P]], channel_multiplier=1).then_inc(setup, 1)

            def split(n, s, i):
                pool.wait_ge(raw_in[s], 16 * (i + 1))
                need(pool, half_done, 2 * n - 2)
                stand(pool, pool_passed)
                pool.tensor_scalar(wsp[:, s, 0, :], raw[:, s, :], 1.0, 0.0, ALU.mult, ALU.add).then_inc(w_high, 1)
                need(pool, w_high, n + 1)
                pool.tensor_tensor(wsp[:, s, 1, :], raw[:, s, :], wsp[:, s, 0, :].bitcast(F32),
                                   ALU.subtract).then_inc(w_ready, 1)

            def normalise(parts, ring, u):
                need(pool, inverted, u + 1)
                stand(pool, pool_passed)
                for hh, part in enumerate(parts):
                    ins = pool.tensor_scalar(part, part, rden[:, ring, hh:hh + 1], 0.0, ALU.mult, ALU.add)
                ins.then_inc(normed, 1)

            def splits(first, last):
                with pool.Fori(first // 2, last // 2) as i:
                    for s in range(2):
                        split(2 * i + s, s, i)

            def add_squares(bi, half):
                tiles = added(bi, half)
                into = square(bi, half, tiles[0])
                done = sums(bi, half) - len(tiles) + 1
                for k in tiles[1:]:
                    need(pool, sq_made, 16 * bi + 8 * half + k + 1)
                    need(pool, sq_summed, done)
                    pool.tensor_tensor(into, into, square(bi, half, k), ALU.add).then_inc(sq_summed, 1)
                    done += 1

            def boundary(bi, n):
                split(n, 0, n // 2)
                add_squares(bi, 0)
                split(n + 1, 1, n // 2)
                add_squares(bi, 1)

            splits(0, QKV0)
            boundary(1, QKV0)
            splits(QKV0 + 2, QKV0 + 6)

            THRESHOLDS = STARTS[1:] + [WINDOW]
            HEAD_STEPS = 4 * (BUCKETS + 1)
            BLOCK_STEPS = 8 + 2 * len(THRESHOLDS) + HEAD_STEPS

            def general_bias(b):
                base = 1 + BLOCK_STEPS * b
                n = 0

                def step(ins):
                    nonlocal n
                    n += 1
                    ins.then_inc(gen, 1)
                    pool.wait_ge(gen, base + n)
                    stand(pool, pool_passed)

                pool.dma_start(krow, bass.AP(pos_dram, b * P, [[0, P], [POS_ROW, 2], [1, 2 * P]])
                               ).then_inc(rows_in, 16)
                with nc.allow_non_contiguous_dma(reason="a position per partition"):
                    pool.dma_start(qcol, bass.AP(pos_dram, P + b * P, [[1, P], [POS_ROW, 2]])).then_inc(rows_in, 16)
                pool.wait_ge(rows_in, 16 + 32 * (b + 1))
                stand(pool, pool_passed)
                for c, part in enumerate((rel, hit)):
                    step(pool.tensor_scalar(part, krow[:, c, :], qcol[:, c:c + 1], -1.0, ALU.subtract, ALU.mult))
                step(pool.tensor_scalar(bkt, rel, -0.5 * POS_HIGH, float(POS_HIGH), ALU.is_lt, ALU.mult))
                step(pool.tensor_tensor(rel, rel, bkt, ALU.add))
                step(pool.tensor_scalar(rel, rel, float(POS_HIGH), 0.0, ALU.mult, ALU.add))
                step(pool.tensor_tensor(rel, rel, hit, ALU.add))
                step(pool.tensor_scalar(bkt, rel, 0.0, float(BUCKETS), ALU.is_lt, ALU.mult))
                for start in THRESHOLDS:
                    step(pool.tensor_scalar(hit, rel, float(start), 1.0, ALU.is_ge, ALU.mult))
                    step(pool.tensor_tensor(bkt, bkt, hit, ALU.add))
                step(pool.memset(acc, 0.0))
                with pool.Fori(0, BUCKETS + 1) as r:
                    at = base + n + 4 * r
                    pool.tensor_scalar(one_of, bkt, 0.0, 1.0, ALU.is_equal, ALU.mult).then_inc(gen, 1)
                    pool.wait_ge(gen, at + 1)
                    stand(pool, pool_passed)
                    pool.tensor_tensor(prod, one_of.rearrange("p (a k) -> p a k", a=1).to_broadcast([P, HEADS, 2 * P]),
                                       trow[:, bass.ds(r * HEADS, HEADS)].rearrange("p (h a) -> p h a", a=1)
                                       .to_broadcast([P, HEADS, 2 * P]), ALU.mult).then_inc(gen, 1)
                    pool.wait_ge(gen, at + 2)
                    pool.tensor_tensor(acc, acc, prod, ALU.add).then_inc(gen, 1)
                    pool.tensor_scalar(bkt, bkt, -1.0, 0.0, ALU.add, ALU.add).then_inc(gen, 1)
                    pool.wait_ge(gen, at + 4)
                    stand(pool, pool_passed)
                n += HEAD_STEPS
                pool.wait_ge(gen, base + n)
                pool.dma_start(region(b, 0, P, P, [[RUN, HEADS], [1, 2 * P]]), acc).then_inc(region_out, 16)
                pool.wait_ge(region_out, 16 * (b + 1))
                stand(pool, pool_passed)

            pool.wait_ge(pos_halves, POS_STEPS)
            pool.wait_ge(bias_made, 16 * 6)
            pool.wait_ge(pos_saved, 16 * 4)
            pool.wait_ge(x_saved, 16)
            need(pool, h_low, 32)
            with pool.If(pool.value_load(flags[0:1, 0:1], min_val=0, max_val=1) > 0):
                pool.memset(trow[:, BUCKETS * HEADS:(BUCKETS + 1) * HEADS], NEG_INF).then_inc(gen, 1)
                pool.dma_start(trow[:, 0:BUCKETS * HEADS], bass.AP(table.tensor, 0, [[0, P], [1, BUCKETS * HEADS]])
                               ).then_inc(rows_in, 16)
                with pool.Fori(0, NB) as b:
                    general_bias(b)
                pool.sem_inc(tables_done, 1)
            with pool.Else():
                pool.sem_inc(tables_done, 1)

            splits(QKV0 + 6, CONV0)


            def swa_slot(i, t):
                if r := prepared(i, t, 1):
                    g, b, par, pr = r
                    blk = bass.ds(b * P, P)
                    need(pool, qs_high, g + 1)
                    stand(pool, pool_passed)
                    pool.tensor_tensor(qs[:, 1, 4 * pr:4 * pr + 4, :], qkv[:, 4 * pr:4 * pr + 4, blk],
                                       qs[:, 0, 4 * pr:4 * pr + 4, :].bitcast(F32), ALU.subtract).then_inc(qs_low, 1)
                    if isinstance(i, int) and 16 * i + t == -3:
                        for s in range(2):
                            split(CONV0 + s, s, CONV0 // 2)
                if r := unit(i, t - 1):
                    u, b, par, j = r
                    normalise([sc[:, j % 4, hh, 0:2 * P] for hh in range(2)], j % 4, u)

            windows(pool, swa_slot)
            splits(CONV0 + 2, Q0)
            boundary(2, Q0)
            splits(Q0 + 2, O0)

            for t in range(-4, 16 + LAG):
                if 0 <= (w := t - 1) < 16:
                    normalise([sx[:, w % 2, qb * 256:(qb + 1) * 256] for qb in range(2)], w % 4, UNITS + w)
                if 0 <= (w := t + 3) < 16:
                    need(pool, xq_high, w + 1)
                    pool.tensor_tensor(qx[:, w % 2, 1, :, :], xq(w), qx[:, w % 2, 0, :, :].bitcast(F32),
                                       ALU.subtract).then_inc(xq_low, 1)
                if t in (13, 15):
                    split(O0 + (t - 13) // 2, (t - 13) // 2, O0 // 2)

            splits(O0 + 2, FFN2)
            boundary(3, FFN2)
            splits(FFN2 + 2, BLOCKS)
            for half in range(2):
                add_squares(4, half)
            for half in range(2):
                need(pool, rstd_made, 8 + half + 1)
                for n, k in enumerate(POOL_OUT[half]):
                    pool.wait_ge(out_scaled[half], n + 1)
                    pool.tensor_tensor(qkv[:, k, hs(half)], x[:, k, hs(half)], rstd[:, hs(half)], ALU.mult
                                       ).then_inc(outs_pool, 1)

        @block.tensor
        def _(pe):
            credits(pe, "pe")

            def three(o, lhs, rhs, start, stop):
                pe.matmul(o, lhs[0], rhs[0], start=start, stop=False)
                pe.matmul(o, lhs[0], rhs[1], start=False, stop=False)
                return pe.matmul(o, lhs[1], rhs[0], start=False, stop=stop)

            def wtile(n, m):
                s = n % 2
                return [wsp[:, s, part, m * P:(m + 1) * P] for part in range(2)]

            def column(n, s, bank, read, use, boundary=None, after=None):
                need(pe, w_ready, n + 1)
                for half in range(2):
                    need(pe, read, 2 * use + half - 1)
                    if after is not None:
                        need(pe, root, 2 * after + half + 1)
                    for k in range(DT):
                        if after and (half, k) == (0, DT - 2):
                            squares(after, 1)
                        if boundary is not None:
                            need(pe, h_low, 16 * boundary + 8 * half + k + 1)
                        ins = three(bank[:, half, :], wtile(s, k), [h[:, part, k, hs(half)] for part in range(2)],
                                    k == 0, k == DT - 1)
                    ins.then_inc(half_done, 1)
                    if boundary and half == 0:
                        squares(boundary, 0)

            def rows(n, s, dn, rhs, ready=None):
                need(pe, w_ready, n + 1)
                for r in range(16):
                    half, m = r // 8, r % 8
                    if ready is not None and m == 0:
                        ready(half)
                    need(pe, x_added, 16 * dn + r - 3)
                    ins = three(psD[:, r % 4, :], wtile(s, m), rhs(half), True, True)
                    ins.then_inc(half_done if m == 7 else d_full, 1)

            def squares(bi, half, left=True):
                if left:
                    squares_left(bi, half)
                need(pe, sq_summed, sums(bi, half))
                at = added(bi, half)[0]
                pe.matmul(psB[:, half, :], mean[:, :], square(bi, half, at), start=(at == 0), stop=True
                          ).then_inc(ss_full, 1)

            def squares_left(bi, half):
                for k in range(added(bi, half)[0]):
                    need(pe, sq_made, 16 * bi + 8 * half + k + 1)
                    pe.matmul(psB[:, half, :], mean[:, :], square(bi, half, k), start=(k == 0), stop=False)

            pe.wait_ge(tab_in, 32)
            pe.wait_ge(vec_setup, 1)
            pe.matmul(psD[0:HEADS, 0, 0:RUN], tab[:, :], hot, start=True, stop=True).then_inc(vrow_mm, 1)

            pe.wait_ge(setup, 4)
            for k in range(DT):
                pe.wait_ge(m_sq, k + 1)
                pe.matmul(psD[:, 1, 0:M], mean[:, :], sq[:, k % 2, 0:M], start=(k == 0), stop=(k == DT - 1)
                          ).then_inc(m_ss, 1)
            pe.wait_ge(m_low, DT)

            def kv_block(n, s, bank, read, use):
                need(pe, w_ready, n + 1)
                need(pe, read, use)
                for k in range(DT):
                    ins = three(bank[:, 0, 0:M], wtile(s, k), [memh[:, part, k, :] for part in range(2)],
                                k == 0, k == DT - 1)
                ins.then_inc(half_done, 2)

            def turn_values(t):
                need(pe, (a_read, b_read)[t % 2], (DT + t) // 2 + 1)
                for mt in range(2):
                    n = 2 * t + mt
                    if n >= 2:
                        pe.wait_ge(m_copied, n - 1)
                    pe.transpose(psD[:, 2 + n % 2, 0:P], kvT[:, DT + t, mt * P:(mt + 1) * P], ident[:, :]
                                 ).then_inc(m_turned, 1)

            for n in range(KV_BLOCKS):
                kv_block(n, n % 2, (psA, psB)[n % 2], (a_read, b_read)[n % 2], n // 2)
                if n == 0:
                    pe.wait_ge(vrow_cp, 1)
                if n == DT:
                    pe.wait_ge(m_root, 1)
                need(pe, sq_made, n + 1)
                pe.matmul(psD[:, n // DT, :], mean[:, :], square(0, n // DT, n % DT), start=(n % DT == 0),
                          stop=(n % DT == DT - 1)).then_inc(ss_full, 1)
                if n >= DT + 2:
                    turn_values(n - DT - 2)
            turn_values(DT - 2)
            turn_values(DT - 1)

            def use_a(u):
                return u - 4

            def use_b(u):
                return u - 4

            def ffn(n0, a0, b0, d0, bi):
                def act_rhs(half):
                    return [act[:, part, hs(half)] for part in range(2)]

                def act_ready(t):
                    def wait(half):
                        need(pe, act_low, 2 * t + half + 1)
                    return wait

                t0 = FFN1_T if bi == 0 else FFN2_T
                column(n0, n0, psA, a_read, use_a(a0), boundary=bi)
                column(n0 + 1, n0 + 1, psB, b_read, use_b(b0), after=bi)

                def body(t, n, s):
                    column(n, s, psA, a_read, use_a(a0) + t)
                    rows(n + 1, s + 1, d0 + t - 1, act_rhs, act_ready(t0 + t - 1))
                    column(n + 2, s, psB, b_read, use_b(b0) + t)

                with pe.Fori(0, (FT - 2) // 2) as i:
                    body(2 * i + 1, n0 + 2 + 6 * i, n0)
                    body(2 * i + 2, n0 + 5 + 6 * i, n0 + 1)
                body(FT - 1, n0 + 2 + 3 * (FT - 2), n0)
                rows(n0 + 3 * FT - 1, n0 + 1, d0 + FT - 1, act_rhs, act_ready(t0 + FT - 1))

            need(pe, a_read, 8)
            need(pe, b_read, 8)
            pe.wait_ge(m_copied, 16)
            ffn(FFN1, FFN1_A, FFN1_B, FFN1_D, 0)

            need(pe, b_read, 2 * use_b(QKV_B))
            column(QKV0, 0, psA, a_read, use_a(QKV_A), boundary=1)
            column(QKV0 + 1, 1, psB, b_read, use_b(QKV_B), after=1)
            with pe.Fori(1, QKV_BLOCKS // 2) as i:
                column(QKV0 + 2 * i, 0, psA, a_read, use_a(QKV_A) + i)
                column(QKV0 + 2 * i + 1, 1, psB, b_read, use_b(QKV_B) + i)

            need(pe, a_read, 2 * use_a(CONV_A))
            need(pe, b_read, 2 * use_b(CONV_B))
            need(pe, x_added, 16 * CONV_D)

            def swa_slot(i, t):
                if r := prepared(i, t, 2):
                    g, b, par, pr = r
                    need(pe, vst_made, g + 1)
                    need(pe, vv_low, g)
                    pe.transpose(psV, vst[:, pr, :], ident[:, :]).then_inc(v_turned, 1)
                if r := unit(i, t + 1):
                    u, b, par, j = r
                    if j % 4 == 0:
                        need(pe, qs_low, 4 * i + (t + 1) // 4 + 1)
                        need(pe, kz_low, 8 * i + 2 * ((t + 1) // 4) + 2)
                    need(pe, scored, u - (1 if j % 2 else 3))
                    three(psQ(j), [qs[:, part, j, :] for part in range(2)],
                          [kz[:, part, j // 4, :, :, :].rearrange("p g s k -> p (g s k)") for part in range(2)],
                          True, True).then_inc(qk_done, 1)
                if r := unit(i, t - 3):
                    u, b, par, j = r
                    need(pe, pt_low, u + 1)
                    if j % 4 == 0:
                        need(pe, vv_low, 4 * i + (t - 3) // 4 + 1)
                    need(pe, o_out, u - 1)
                    pr = j // 4
                    for slot in range(2):
                        ins = three(psO(j)[:, 0:256], [vv[:, part, slot, pr * P:(pr + 1) * P] for part in range(2)],
                                    [pt[:, j % 2, part, slot, :] for part in range(2)], slot == 0, slot == 1)
                    ins.then_inc(pv_done, 1)
                if r := unit(i, t - 1):
                    u, b, par, j = r
                    need(pe, normed, u + 1)
                    need(pe, pt_low, u - 1)
                    for slot in range(2):
                        for hh in range(2):
                            ins = pe.transpose(psT(j)[:, slot * 256 + hh * P:slot * 256 + (hh + 1) * P],
                                               sc[:, j % 4, hh, slot * P:(slot + 1) * P], ident[:, :])
                    ins.then_inc(turned, 1)

            windows(pe, swa_slot)

            need(pe, scored, UNITS)
            need(pe, o_out, UNITS)

            def mrg_rhs(half):
                return [mrg[:, part, hs(half)] for part in range(2)]

            def mrg_ready(t):
                def wait(half):
                    need(pe, act_low, 2 * (CONV_T + t) + half + 1)
                return wait

            A, B = use_a(CONV_A), use_b(CONV_B)

            def conv_tile(t, n, s, peeled):
                column(n, s, psA, a_read, A + 3 * t)
                column(n + 1, s + 1, psB, b_read, B + 2 * t)
                k = 2
                if not peeled:
                    rows(n + 2, s, CONV_D + t - 1, mrg_rhs, mrg_ready(t - 1))
                    k = 3
                column(n + k, s + k, psA, a_read, A + 3 * t + 1)
                column(n + k + 1, s + k + 1, psB, b_read, B + 2 * t + 1)
                column(n + k + 2, s + k + 2, psA, a_read, A + 3 * t + 2)

            conv_tile(0, CONV0, CONV0, True)
            with pe.Fori(1, DT) as t:
                conv_tile(t, CONV0 - 1 + 6 * t, CONV0 + 5, False)
            rows(Q0 - 1, Q0 - 1, CONV_D + DT - 1, mrg_rhs, mrg_ready(DT - 1))

            need(pe, b_read, 2 * use_b(Q_B))
            column(Q0, 0, psA, a_read, use_a(Q_A), boundary=2)
            column(Q0 + 1, 1, psB, b_read, use_b(Q_B), after=2)
            with pe.Fori(1, Q_BLOCKS // 2) as i:
                column(Q0 + 2 * i, 0, psA, a_read, use_a(Q_A) + i)
                column(Q0 + 2 * i + 1, 1, psB, b_read, use_b(Q_B) + i)
            need(pe, a_read, 2 * use_a(FFN2_A))
            need(pe, b_read, 2 * use_b(FFN2_B))

            need(pe, x_added, 16 * O_D)

            for t in range(-4, 16 + LAG):
                if 0 <= (w := t + 2) < 16:
                    k = kx[w // 4 % 2]
                    need(pe, kxl, 2 * (w // 4) + 1)
                    need(pe, xq_low, w + 1)
                    need(pe, exp_done, UNITS + w - 3)
                    for qb in range(2):
                        for kt in range(2):
                            ins = three(psS(w)[:, qb * 256:(qb + 1) * 256],
                                        [qx[:, w % 2, part, kt, qb * P:(qb + 1) * P] for part in range(2)],
                                        [k[:, part, kt, :] for part in range(2)], kt == 0, kt == 1)
                    ins.then_inc(qk_done, 1)
                if 0 <= (w := t - 3) < 16:
                    v = vx[w // 4 % 2]
                    need(pe, kxl, 2 * (w // 4) + 2)
                    need(pe, pt_low, UNITS + w + 1)
                    need(pe, xo_low, w - 1)
                    for dt in range(2):
                        for mt in range(2):
                            ins = three(psO(w)[:, dt * 256:(dt + 1) * 256],
                                        [v[:, part, mt, dt * P:(dt + 1) * P] for part in range(2)],
                                        [px[:, w % 2, part, mt, :] for part in range(2)], mt == 0, mt == 1)
                    ins.then_inc(pv_done, 1)
                if 0 <= (w := t - 1) < 16:
                    need(pe, normed, UNITS + w + 1)
                    need(pe, pt_low, UNITS + w - 1)
                    for mt in range(2):
                        for qb in range(2):
                            ins = pe.transpose(psT(w)[:, mt * 256 + qb * P:mt * 256 + (qb + 1) * P],
                                               sx[:, w % 2, qb * 256 + mt * P:qb * 256 + (mt + 1) * P], ident[:, :])
                    ins.then_inc(turned, 1)

            need(pe, xo_low, 16)
            with pe.Fori(0, O_BLOCKS // 2) as i:
                for s in range(2):
                    rows(O0 + 2 * i + s, s, O_D + 2 * i + s, lambda half: [
                        h[:, part, bass.ds(2 * i + s, 1), hs(half)].rearrange("p a s -> p (a s)")
                        for part in range(2)])

            ffn(FFN2, FFN2_A, FFN2_B, FFN2_D, 3)
            need(pe, b_read, 2 * (use_b(FFN2_B) + FT))
            squares_left(4, 1)
            squares(4, 0)
            squares(4, 1, left=False)

        @block.scalar
        def _(act_e):
            e = act_e
            credits(e, "act")
            e.dma_start(gn[:, :, :], gains).then_inc(gains_in, 16)
            e.dma_start(tab[0:BUCKETS, :], table).then_inc(tab_in, 16)
            e.dma_start(hot, onehot).then_inc(tab_in, 16)
            e.dma_start(cw[:, :, :], conv_w).then_inc(const_in, 16)
            e.dma_start(snk[:, :], bass.AP(sinks.tensor, 0, [[0, P], [1, HEADS]])).then_inc(const_in, 16)
            for k in range(DT):
                e.dma_start(x[:, k, :], xT[:, k, :]).then_inc(x_in[k // 4], 16)
            e.wait_ge(gains_in, 16)
            for k in range(DT):
                if k % 4 == 0:
                    e.wait_ge(mem_in[k // 4], 16)
                e.activation(memh[:, 0, k, :], mem[:, k, :], ACT.Copy, scale=gn[:, 4, k:k + 1]).then_inc(m_high, 1)
                if k >= 2:
                    e.wait_ge(m_ss, k - 1)
                e.activation(sq[:, k % 2, 0:M], mem[:, k, :], ACT.Square).then_inc(m_sq, 1)
            e.wait_ge(m_ss, DT)
            e.wait_ge(vec_setup, 2)
            e.activation(rstd[:, 0:M], psD[:, 1, 0:M], ACT.Sqrt, bias=epst[:, 0:1]).then_inc(m_root, 1)

            def bias_by_distance():
                e.wait_ge(vrow_cp, 1)
                e.dma_start(bass.AP(vrow_dram, 0, [[RUN, HEADS], [1, RUN]]), vrow).then_inc(vrow_out, 16)

            def bias_shifted():
                e.wait_ge(vrow_out, 16)
                e.dma_start(bass.AP(bias_dram, REGION, [[ROWLEN + 1, P], [1, ROWLEN]]),
                            bass.AP(vrow_dram, 0, [[0, P], [1, ROWLEN]])).then_inc(bias_made, 16)
                e.wait_ge(setup, 4)
                for q in range(4):
                    e.dma_start(region(0, 0, P, P + q * 4 * RUN, [[RUN, 4], [1, P]]),
                                negt.rearrange("p (a k) -> p a k", a=1).to_broadcast([P, 4, P])
                                ).then_inc(bias_made, 16)

            def bias_block0():
                e.wait_ge(bias_made, 16 * 5)
                e.dma_start(region(0, 0, P, 2 * P, [[RUN, HEADS], [1, P]]),
                            region(1, 0, P, 2 * P, [[RUN, HEADS], [1, P]])).then_inc(bias_made, 16)

            def warm(n, function):
                e.activation(warmed[:, n:n + 1], epst[:, 0:1], function)

            def high(bi, half, k, gain):
                e.activation(h[:, 0, k, hs(half)], x[:, k, hs(half)], ACT.Copy,
                             scale=gn[:, gain, k:k + 1]).then_inc(h_high, 1)

            def squares(bi, half, k):
                if bi == 0:
                    need(e, ss_full, 8 * half + k - 1)
                e.activation(square(bi, half, k), x[:, k, hs(half)], ACT.Square).then_inc(sq_made, 1)

            def roots(bi):
                for half in range(2):
                    if (bi, half) == (4, 1):
                        for k in POOL_OUT[0][2:]:
                            out_gain(0, k)
                    need(e, ss_full, ss_event(bi, half))
                    e.activation(rstd[:, hs(half)], (psD if bi == 0 else psB)[:, half, :], ACT.Sqrt,
                                 bias=epst[:, 0:1]).then_inc(root, 1)

            def out_gain(half, k):
                e.activation(x[:, k, hs(half)], x[:, k, hs(half)], ACT.Copy, scale=gn[:, 5, k:k + 1]
                             ).then_inc(out_scaled[half], 1)

            def boundary(bi, dn, gain):
                for half in range(2):
                    for k in range(DT):
                        if dn is not None:
                            need(e, x_added, 16 * dn + 8 * half + k + 1)
                        if gain is not None:
                            high(bi, half, k, gain)
                        squares(bi, half, k)
                if gain is None:
                    for k in POOL_OUT[0][:2]:
                        out_gain(0, k)
                roots(bi)

            e.wait_ge(const_in, 32)
            bias_by_distance()
            e.wait_ge(m_ss, DT)
            for half in range(2):
                for k in range(DT):
                    if half == 0 and k % 4 == 0:
                        e.wait_ge(x_in[k // 4], 16 * 4)
                    squares(0, half, k)
                    high(0, half, k, 0)
            need(e, a_read, 8)
            need(e, b_read, 8)
            roots(0)
            e.wait_ge(m_copied, 16)
            e.dma_start(kv_dram[:, 0:2, :], qkv[:, 0:2, :]).then_inc(kv_saved, 16)
            e.dma_start(kv_dram[:, 2:4, :], vnat).then_inc(kv_saved, 16)
            e.dma_start(ipos, positions).then_inc(pos_in, 16)
            bias_shifted()

            def ffn(s0, a0, t0, first, last):
                with e.Fori(first, last) as t:
                    for half in range(2):
                        need(e, a_read, 2 * (a0 - 4 + t) + half + 1)
                        e.activation(gate[:, hs(half)], gate[:, hs(half)], ACT.Silu).then_inc(silu_done, 1)
                    for half in range(2):
                        need(e, act_mid, 2 * (t0 + t) + half + 1)
                        e.activation(act[:, 0, hs(half)], up[:, hs(half)], ACT.Copy).then_inc(act_high, 1)

            ffn(0, FFN1_A, FFN1_T, 0, 4)
            bias_block0()
            ffn(0, FFN1_A, FFN1_T, 4, FT)
            e.wait_ge(kv_saved, 32)
            boundary(1, FFN1_D + FT - 1, 1)
            need(e, x_added, 16 * CONV_D)
            e.dma_start(x_dram[:, :, :], x[:, :, :]).then_inc(x_saved, 16)
            e.wait_ge(pos_halves, POS_STEPS)
            for c in range(2):
                e.dma_start(bass.AP(pos_dram, c * POS_ROW, [[P, 1], [1, P]]), fpad[c]).then_inc(pos_saved, 16)
                e.dma_start(bass.AP(pos_dram, c * POS_ROW + P, [[S, 1], [1, S]]), fpos[c]).then_inc(pos_saved, 16)
            e.wait_ge(x_saved, 16)
            need(e, h_low, 32)
            e.wait_ge(tables_done, 1)

            warm(0, ACT.Exp)
            need(e, a_read, 2 * (QKV_A - 4 + DT // 2 + 1))
            need(e, b_read, 2 * (QKV_B - 4 + DT // 2 + 1))

            def swa_slot(i, t):
                if r := prepared(i, t, 3):
                    g, b, par, pr = r
                    need(e, v_turned, g + 1)
                    need(e, pv_done, 4 * g - 4)
                    e.activation(vv[:, 0, par, pr * P:(pr + 1) * P], psV, ACT.Copy).then_inc(vv_high, 1)
                if r := unit(i, t):
                    u, b, par, j = r
                    need(e, maxed, u + 1)
                    for hh in range(2):
                        part = sc[:, j % 4, hh, 0:2 * P + 1]
                        ins = e.activation(part, part, ACT.Exp, bias=nmx[:, j % 4, hh:hh + 1],
                                           accum_out=rs[:, j % 4, hh:hh + 1])
                    ins.then_inc(exp_done, 1)
                if r := prepared(i, t, 0):
                    g, b, par, pr = r
                    blk = bass.ds(b * P, P)
                    need(e, qk_done, 4 * g - 4)
                    stand(e, act_passed)
                    e.activation(qs[:, 0, 4 * pr:4 * pr + 4, :], qkv[:, 4 * pr:4 * pr + 4, blk], ACT.Copy
                                 ).then_inc(qs_high, 1)
                    for kh in range(2):
                        own = slice(kh * HD, (kh + 1) * HD)
                        e.activation(kz[own, 0, pr, kh, par, :], qkv[own, 8 + pr, blk], ACT.Copy).then_inc(kz_high, 1)
                    need(e, v_turned, g - 1)
                    if isinstance(i, int):
                        need(e, a_read, 2 * (CONV_A - 4))
                        need(e, b_read, 2 * (CONV_B - 4))
                    stand(e, act_passed)
                    e.activation(vst[:, pr, :], qkv[:, 10 + pr, blk], ACT.Copy).then_inc(vst_made, 1)
                if r := unit(i, t - 2):
                    u, b, par, j = r
                    need(e, turned, u + 1)
                    need(e, pv_done, u - 1)
                    e.activation(pt[:, j % 2, 0, :, :].rearrange("p s k -> p (s k)"), psT(j), ACT.Copy
                                 ).then_inc(pt_high, 1)
                if r := unit(i, t - 4):
                    u, b, par, j = r
                    need(e, pv_done, u + 1)
                    stand(e, act_passed)
                    for hh in range(2):
                        ins = e.activation(qkv[hh * HD:(hh + 1) * HD, j, bass.ds(b * P, P)],
                                           psO(j)[hh * HD:(hh + 1) * HD, hh * P:(hh + 1) * P], ACT.Copy)
                    ins.then_inc(o_out, 1)

            windows(e, swa_slot)

            need(e, pv_done, UNITS)
            e.dma_start(x[:, :, :], x_dram[:, :, :]).then_inc(x_back, 16)

            def conv_tile(t):
                need(e, conv_v, 12 * t + 2)
                stand(e, act_passed)
                tap = cw[:, bass.ds(t, 1), 0:1].rearrange("p a b -> p (a b)")
                for half in range(2):
                    e.activation(cv[:, hs(half)], cu[:, half * HALF:(half + 1) * HALF], ACT.Copy, scale=tap
                                 ).then_inc(conv_s, 1)
                for half in range(2):
                    need(e, b_read, 2 * (CONV_B - 4 + 2 * t + 1) + half + 1)
                    e.activation(cG[:, hs(half)], cG[:, hs(half)], ACT.Sigmoid).then_inc(conv_s, 1)
                for half in range(2):
                    need(e, a_read, 2 * (CONV_A - 4 + 3 * t + 2) + half + 1)
                    e.activation(cA[:, hs(half)], cA[:, hs(half)], ACT.Sigmoid).then_inc(conv_s, 1)
                    need(e, act_mid, 2 * (CONV_T + t) + half + 1)
                    e.activation(mrg[:, 0, hs(half)], cB[:, hs(half)], ACT.Copy).then_inc(act_high, 1)

            with e.Fori(0, DT) as t:
                conv_tile(t)
            need(e, act_low, 2 * (CONV_T + DT))
            e.dma_start(qkv[:, 8:12, :], kv_dram[:, :, :]).then_inc(kv_back, 16)
            boundary(2, CONV_D + DT - 1, 2)

            e.wait_ge(kv_back, 16)
            warm(1, ACT.Exp)

            for t in range(-4, 16 + LAG):
                if t % 4 == 0 and 0 <= (hd := t // 4 + 1) < MEM_HEADS:
                    need(e, qk_done, UNITS + 4 * (hd - 1) if hd >= 2 else 0)
                    if hd == 1:
                        need(e, a_read, 2 * (FFN2_A - 4))
                        need(e, b_read, 2 * (FFN2_B - 4))
                    e.activation(kx[hd % 2][:, 0, :, :], kmem[:, 2 * hd:2 * hd + 2, :], ACT.Copy).then_inc(kxs, 1)
                if t % 4 == 3 and 0 <= (hd := t // 4 + 1) < MEM_HEADS:
                    need(e, pv_done, UNITS + 4 * (hd - 1) if hd >= 2 else 0)
                    e.activation(vx[hd % 2][:, 0, :, :], vmem[:, :, hd * MHD:(hd + 1) * MHD], ACT.Copy
                                 ).then_inc(kxs, 1)
                if 0 <= (w := t) < 16:
                    need(e, maxed, UNITS + w + 1)
                    need(e, turned, UNITS + w - 1 if w >= 2 else 0)
                    for qb in range(2):
                        ins = e.activation(sx[:, w % 2, qb * 256:(qb + 1) * 256], psS(w)[:, qb * 256:(qb + 1) * 256],
                                           ACT.Exp, bias=nmx[:, w % 4, qb:qb + 1], accum_out=rs[:, w % 4, qb:qb + 1])
                    ins.then_inc(exp_done, 1)
                if 0 <= (w := t + 3) < 16:
                    need(e, qk_done, UNITS + w - 1 if w >= 2 else 0)
                    need(e, a_read, 2 * (Q_A - 4 + w // 4 + 1))
                    need(e, b_read, 2 * (Q_B - 4 + w // 4 + 1))
                    e.activation(qx[:, w % 2, 0, :, :], xq(w), ACT.Copy).then_inc(xq_high, 1)
                if 0 <= (w := t - 2) < 16:
                    need(e, turned, UNITS + w + 1)
                    need(e, pv_done, UNITS + w - 1)
                    e.activation(px[:, w % 2, 0, :, :].rearrange("p s k -> p (s k)"), psT(w), ACT.Copy
                                 ).then_inc(pt_high, 1)
                if 0 <= (w := t - 4) < 16:
                    need(e, pv_done, UNITS + w + 1)
                    e.activation(h[:, 0, 2 * (w // 4):2 * (w // 4) + 2, w % 4 * 256:(w % 4 + 1) * 256],
                                 psO(w).rearrange("p (d q) -> p d q", d=2), ACT.Copy).then_inc(xo_high, 1)

            boundary(3, O_D + DT - 1, 3)
            ffn(FT, FFN2_A, FFN2_T, 0, FT)
            boundary(4, FFN2_D + FT - 1, None)
            for k in POOL_OUT[1]:
                out_gain(1, k)
            for half, pairs in enumerate(((0, 4, 2, 6), (0, 2, 6, 4))):
                for k in pairs:
                    if k in POOL_OUT[half]:
                        e.wait_ge(outs_pool, POOL_OUT[half].index(k) + 2 + half * len(POOL_OUT[0]))
                    else:
                        e.wait_ge(outs, k + 2 + half * (DT - len(POOL_OUT[0])))
                    e.dma_start(out[:, k:k + 2, hs(half)], qkv[:, k:k + 2, hs(half)]).then_inc(out_done, 16)
            e.wait_ge(out_done, 16 * DT)

        @block.vector
        def _(v_e):
            e = v_e
            credits(e, "dve")
            e.memset(tab[BUCKETS:BUCKETS + 1, :], NEG_INF).then_inc(vec_setup, 1)
            e.memset(epst[:, :], EPS).then_inc(vec_setup, 1)
            e.wait_ge(vrow_mm, 1)
            e.tensor_copy(vrow, psD[0:HEADS, 0, 0:RUN]).then_inc(vrow_cp, 1)
            e.wait_ge(gains_in, 16)
            for k in range(DT):
                e.wait_ge(m_high, k + 1)
                e.scalar_tensor_tensor(out=memh[:, 1, k, :], in0=mem[:, k, :], scalar=gn[:, 4, k:k + 1],
                                       in1=memh[:, 0, k, :].bitcast(F32), op0=ALU.mult, op1=ALU.subtract
                                       ).then_inc(m_low, 1)

            e.wait_ge(m_root, 1)
            e.reciprocal(rstd[:, 0:M], rstd[:, 0:M]).then_inc(m_rstd, 1)
            e.wait_ge(m_rstd, 1)
            def low(bi, half, k, gain):
                r = 16 * bi + 8 * half + k
                need(e, h_high, r + 1)
                e.scalar_tensor_tensor(out=h[:, 1, k, hs(half)], in0=x[:, k, hs(half)], scalar=gn[:, gain, k:k + 1],
                                       in1=h[:, 0, k, hs(half)].bitcast(F32), op0=ALU.mult, op1=ALU.subtract
                                       ).then_inc(h_low, 1)

            def rstds(bi):
                for half in range(2):
                    one_rstd(bi, half)
                need(e, rstd_made, 2 * bi + 2)

            def one_rstd(bi, half):
                need(e, root, 2 * bi + half + 1)
                e.reciprocal(rstd[:, hs(half)], rstd[:, hs(half)]).then_inc(rstd_made, 1)

            def add(n, dn, r, scale):
                half, m = r // 8, r % 8
                if m == 7:
                    need(e, half_done, 2 * n + half + 1)
                else:
                    need(e, d_full, 14 * dn + 7 * half + m + 1)
                need(e, x_added, 16 * dn + r - 15)
                e.scalar_tensor_tensor(out=x[:, m, hs(half)], in0=psD[:, r % 4, :], scalar=scale,
                                       in1=x[:, m, hs(half)], op0=ALU.mult, op1=ALU.add).then_inc(x_added, 1)

            def boundary(bi, n, dn, scale, gain):
                for r in range(14):
                    add(n, dn, r, scale)
                for r in range(2):
                    low(bi, 0, r, gain)
                    add(n, dn, 14 + r, scale)
                for r in range(2, 16):
                    low(bi, r // 8, r % 8, gain)
                rstds(bi)

            def copy_values(t):
                for mt in range(2):
                    n = 2 * t + mt
                    e.wait_ge(m_turned, n + 1)
                    e.tensor_copy(vnat[:, mt, t * P:(t + 1) * P], psD[:, 2 + n % 2, 0:P]).then_inc(m_copied, 1)

            for n in range(KV_BLOCKS):
                bank, read = ((psA, a_read), (psB, b_read))[n % 2]
                need(e, half_done, 2 * n + 2)
                e.tensor_tensor(kvT[:, n, :], bank[:, 0, 0:M], rstd[:, 0:M], ALU.mult).then_inc(read, 1)
                if n == 0:
                    e.wait_ge(const_in, 32)
                    e.wait_ge(x_in[0], 16 * 4)
                    e.wait_ge(x_in[1], 16 * 4)
                low(0, n // DT, n % DT, 0)
                if n >= DT + 2:
                    copy_values(n - DT - 2)
            copy_values(DT - 2)
            copy_values(DT - 1)
            rstds(0)

            def look_at_positions():
                steps_done = 0
                e.wait_ge(pos_in, 16)
                e.wait_ge(vrow_out, 16)

                def step(ins):
                    nonlocal steps_done
                    steps_done += 1
                    ins.then_inc(pos_halves, 1)
                    e.wait_ge(pos_halves, steps_done)

                for b in range(NB):
                    ins = e.memset(steps[:, b:b + 1], float(b - 1))
                step(ins)
                step(e.memset(fpad[0], float(POS_PAD // POS_HIGH)))
                step(e.memset(fpad[1], 0.0))
                step(e.tensor_scalar(work[0].bitcast(I32), ipos, 16, None, ALU.arith_shift_right))
                step(e.tensor_scalar(work[1].bitcast(I32), ipos, POS_HIGH - 1, None, ALU.bitwise_and))
                for c in range(2):
                    step(e.tensor_copy(fpos[c], work[c].bitcast(I32)))
                for c in range(2):
                    step(e.tensor_tensor(work[c][:, 1:], fpos[c][:, 1:], fpos[c][:, 0:S - 1], ALU.subtract))
                step(e.scalar_tensor_tensor(out=work[0][:, 1:], in0=work[0][:, 1:], scalar=float(POS_HIGH),
                                            in1=work[1][:, 1:], op0=ALU.mult, op1=ALU.add))
                step(e.tensor_scalar(work[0][:, 1:], work[0][:, 1:], 1.0, None, ALU.not_equal))
                step(e.tensor_reduce(odd[:, 0:1], work[0][:, 1:], AX.X, ALU.max))
                step(e.tensor_scalar(odd[:, 1:2], fpos[0][:, 0:1], float(POS_PAD // POS_HIGH - 1), None, ALU.is_ge))
                step(e.tensor_scalar(odd[:, 2:3], fpos[0][:, 0:1], float(POS_PAD // POS_HIGH), None, ALU.is_le))
                step(e.tensor_tensor(odd[:, 1:2], odd[:, 1:2], odd[:, 2:3], ALU.mult))
                step(e.tensor_tensor(odd[:, 0:1], odd[:, 0:1], odd[:, 1:2], ALU.max))
                step(e.tensor_copy(flags[:, 0:1], odd[:, 0:1]))
                step(e.tensor_scalar(flags[:, 1:], steps[:, :], odd[:, 0:1], 1.0, ALU.mult, ALU.add))


            def ffn(n0, s0, t0, dn0):
                b1 = 2 * ((FFN1_B if n0 == FFN1 else FFN2_B) - 4)
                def gates(t):
                    n = n0 + 3 * t - 1 if not isinstance(t, int) else n0
                    for half in range(2):
                        need(e, half_done, 2 * n + half + 1)
                        e.tensor_tensor(gate[:, hs(half)], psA[:, half, :], rstd[:, hs(half)], ALU.mult
                                        ).then_inc(a_read, 1)

                def ups(t):
                    for half in range(2):
                        need(e, half_done, 2 * (n0 + 3 * t + 1) + half + 1)
                        e.tensor_tensor(up[:, hs(half)], psB[:, half, :], rstd[:, hs(half)], ALU.mult
                                        ).then_inc(b_read, 1)
                        need(e, b_read, b1 + 2 * t + half + 1)
                        need(e, silu_done, 2 * (s0 + t) + half + 1)
                        e.tensor_tensor(up[:, hs(half)], up[:, hs(half)], gate[:, hs(half)], ALU.mult
                                        ).then_inc(act_mid, 1)
                        need(e, act_high, 2 * (t0 + t) + half + 1)
                        need(e, act_mid, 2 * (t0 + t) + half + 1)
                        e.tensor_tensor(act[:, 1, hs(half)], up[:, hs(half)], act[:, 0, hs(half)].bitcast(F32),
                                        ALU.subtract).then_inc(act_low, 1)

                gates(0)
                ups(0)
                with e.Fori(1, FT) as t:
                    gates(t)
                    for r in range(16):
                        add(n0 + 3 * t, dn0 + t - 1, r, 0.5)
                    ups(t)

            ffn(FFN1, 0, FFN1_T, FFN1_D)
            boundary(1, QKV0 - 1, FFN1_D + FT - 1, 0.5, 1)

            def project(i, n0, scale=None):
                for par, (bank, read) in enumerate(((psA, a_read), (psB, b_read))):
                    for half in range(2):
                        need(e, half_done, 2 * (n0 + 2 * i + par) + half + 1)
                        dst = qkv[:, bass.ds(2 * i + par, 1), hs(half)].rearrange("p a s -> p (a s)")
                        if scale is None:
                            e.tensor_tensor(dst, bank[:, half, :], rstd[:, hs(half)], ALU.mult).then_inc(read, 1)
                        else:
                            e.scalar_tensor_tensor(out=dst, in0=bank[:, half, :], scalar=scale,
                                                   in1=rstd[:, hs(half)], op0=ALU.mult, op1=ALU.mult).then_inc(read, 1)

            e.wait_ge(kv_saved, 32)
            e.wait_ge(bias_made, 16 * 6)
            project(0, QKV0, HD ** -0.5)
            look_at_positions()
            e.wait_ge(pos_saved, 16 * 4)
            with e.Fori(1, DT // 2) as i:
                project(i, QKV0, HD ** -0.5)

            e.wait_ge(x_saved, 16)
            e.wait_ge(tables_done, 1)
            for g in range(2):
                e.memset(kz[g * HD:(g + 1) * HD, :, :, 1 - g, :, :].bitcast(F32), 0.0).then_inc(vec_setup, 1)
                e.memset(kz[g * HD:(g + 1) * HD, :, :, g, 1, :].bitcast(F32), 0.0).then_inc(vec_setup, 1)
            e.memset(vv[:, :, 1, :].bitcast(F32), 0.0).then_inc(vec_setup, 1)
            e.wait_ge(vec_setup, 7)

            with e.Fori(DT // 2, QKV_BLOCKS // 2) as i:
                project(i, QKV0)

            def swa_slot(i, t):
                if r := unit(i, t):
                    u, b, par, j = r
                    need(e, qk_done, u + 1)
                    loads = 6 * (i + t // 16) + (4 + j // 4 + 1 if par else 2 * (j // 4 + 1))
                    e.wait_ge(bias_in[j % 4], 16 * loads)
                    e.tensor_tensor(sc[:, j % 4, :, 0:2 * P], psQ(j).rearrange("p (h k) -> p h k", h=2),
                                    bias[:, j % 4, :].rearrange("p (h k) -> p h k", h=2), ALU.add).then_inc(scored, 1)
                if r := unit(i, t - 1):
                    u, b, par, j = r
                    need(e, exp_done, u + 1)
                    e.reciprocal(rden[:, j % 4, :], rs[:, j % 4, :]).then_inc(inverted, 1)
                if r := unit(i, t + 1):
                    u, b, par, j = r
                    need(e, turned, u - 3)
                    e.tensor_copy(sc[:, j % 4, :, 2 * P:2 * P + 1].rearrange("p h a -> p (h a)"),
                                  snk[:, 2 * j:2 * j + 2]).then_inc(sunk, 1)
                if r := unit(i, t):
                    u, b, par, j = r
                    need(e, sunk, u + 1)
                    need(e, scored, u + 1)
                    e.tensor_reduce(nmx[:, j % 4, :], sc[:, j % 4, :, 0:2 * P + 1], AX.X, ALU.max, negate=True
                                    ).then_inc(maxed, 1)
                if r := prepared(i, t, 1):
                    g, b, par, pr = r
                    for kh in range(2):
                        own = slice(kh * HD, (kh + 1) * HD)
                        need(e, kz_high, 2 * g + kh + 1)
                        e.tensor_tensor(kz[own, 1, pr, kh, par, :], qkv[own, 8 + pr, bass.ds(b * P, P)],
                                        kz[own, 0, pr, kh, par, :].bitcast(F32), ALU.subtract).then_inc(kz_low, 1)
                if r := prepared(i, t - 1, 3):
                    g, b, par, pr = r
                    need(e, vv_high, g + 1)
                    e.tensor_tensor(vv[:, 1, par, pr * P:(pr + 1) * P], psV,
                                    vv[:, 0, par, pr * P:(pr + 1) * P].bitcast(F32), ALU.subtract).then_inc(vv_low, 1)
                if r := unit(i, t - 3):
                    u, b, par, j = r
                    need(e, pt_high, u + 1)
                    e.tensor_tensor(pt[:, j % 2, 1, :, :].rearrange("p s k -> p (s k)"), psT(j),
                                    pt[:, j % 2, 0, :, :].rearrange("p s k -> p (s k)").bitcast(F32), ALU.subtract
                                    ).then_inc(pt_low, 1)

            windows(e, swa_slot)

            e.memset(cu[:, 0:2], 0.0).then_inc(vec_setup, 1)
            e.wait_ge(vec_setup, 8)
            need(e, o_out, UNITS)
            a0, b0 = CONV_A - 4, CONV_B - 4

            def conv_tile(t, peeled):
                v = 12 * t
                A, B = a0 + 3 * t, b0 + 2 * t

                n = CONV0 if peeled else CONV0 - 1 + 6 * t
                k = 2 if peeled else 3

                def scaled(dst, bank, read, n, halves=(0, 1)):
                    for half in halves:
                        need(e, half_done, 2 * n + half + 1)
                        e.tensor_tensor(dst[:, hs(half)], bank[:, half, :], rstd[:, hs(half)], ALU.mult
                                        ).then_inc(read, 1)

                scaled(cC, psA, a_read, n)
                scaled(cu[:, 2:], psB, b_read, n + 1)
                need(e, a_read, 2 * A + 2)
                for half in range(2):
                    need(e, b_read, 2 * B + half + 1)
                    seg = cu[:, 2 + half * HALF:2 + (half + 1) * HALF]
                    e.tensor_tensor(seg, seg, cC[:, hs(half)], ALU.mult).then_inc(conv_v, 1)
                if not peeled:
                    for r in range(16):
                        add(n + 2, CONV_D + t - 1, r, 1.0)
                cwt = cw[:, t:t + 1, :] if isinstance(t, int) else cw[:, bass.ds(t, 1), :]
                for tap in (1, 2):
                    for half in range(2):
                        if tap == 1:
                            need(e, conv_s, 6 * t + half + 1)
                            need(e, conv_v, v + 2)
                        else:
                            need(e, conv_v, v + 2 + half + 1)
                        e.scalar_tensor_tensor(out=cv[:, hs(half)],
                                               in0=cu[:, tap + half * HALF:tap + (half + 1) * HALF],
                                               scalar=cwt[:, :, tap:tap + 1].rearrange("p a b -> p (a b)"),
                                               in1=cv[:, hs(half)], op0=ALU.mult, op1=ALU.add).then_inc(conv_v, 1)
                scaled(cB, psA, a_read, n + k)
                need(e, a_read, 2 * (A + 1) + 2)
                for half in range(2):
                    need(e, conv_v, v + 4 + half + 1)
                    e.tensor_tensor(cB[:, hs(half)], cB[:, hs(half)], cv[:, hs(half)], ALU.mult).then_inc(conv_v, 1)
                scaled(cG, psB, b_read, n + k + 1)
                for half in range(2):
                    need(e, conv_s, 6 * t + 2 + half + 1)
                    need(e, conv_v, v + 6 + half + 1)
                    e.tensor_tensor(cB[:, hs(half)], cB[:, hs(half)], cG[:, hs(half)], ALU.mult).then_inc(conv_v, 1)
                att = qkv[:, t, :] if isinstance(t, int) else qkv[:, bass.ds(t, 1), :].rearrange("p a s -> p (a s)")
                for half in range(2):
                    scaled(cA, psA, a_read, n + k + 2, (half,))
                    need(e, conv_s, 6 * t + 4 + half + 1)
                    e.tensor_tensor(cA[:, hs(half)], cA[:, hs(half)], att[:, hs(half)], ALU.mult).then_inc(conv_v, 1)
                    need(e, conv_v, v + 10 + half + 1)
                    e.tensor_tensor(cB[:, hs(half)], cB[:, hs(half)], cA[:, hs(half)], ALU.add).then_inc(act_mid, 1)
                    m = 2 * (CONV_T + t) + half + 1
                    need(e, act_high, m)
                    need(e, act_mid, m)
                    e.tensor_tensor(mrg[:, 1, hs(half)], cB[:, hs(half)], mrg[:, 0, hs(half)].bitcast(F32),
                                    ALU.subtract).then_inc(act_low, 1)

            conv_tile(0, True)
            e.wait_ge(x_back, 16)
            with e.Fori(1, DT) as t:
                conv_tile(t, False)
            boundary(2, Q0 - 1, CONV_D + DT - 1, 1.0, 2)

            with e.Fori(0, Q_BLOCKS // 2) as i:
                project(i, Q0, MHD ** -0.5)
            e.wait_ge(kv_back, 16)

            for t in range(-4, 16 + LAG + 1):
                if t % 4 == 1 and 0 <= (hd := t // 4 + 1) < MEM_HEADS:
                    need(e, kxs, 2 * hd + 1)
                    e.tensor_tensor(kx[hd % 2][:, 1, :, :], kmem[:, 2 * hd:2 * hd + 2, :],
                                    kx[hd % 2][:, 0, :, :].bitcast(F32), ALU.subtract).then_inc(kxl, 1)
                if 0 <= (w := t - 1) < 16:
                    need(e, exp_done, UNITS + w + 1)
                    e.reciprocal(rden[:, w % 4, :], rs[:, w % 4, :]).then_inc(inverted, 1)
                if 0 <= (w := t) < 16:
                    need(e, qk_done, UNITS + w + 1)
                    e.tensor_reduce(nmx[:, w % 4, :], psS(w).rearrange("p (h k) -> p h k", h=2), AX.X, ALU.max,
                                    negate=True).then_inc(maxed, 1)
                if 0 <= (w := t - 3) < 16:
                    need(e, pt_high, UNITS + w + 1)
                    e.tensor_tensor(px[:, w % 2, 1, :, :].rearrange("p s k -> p (s k)"), psT(w),
                                    px[:, w % 2, 0, :, :].rearrange("p s k -> p (s k)").bitcast(F32), ALU.subtract
                                    ).then_inc(pt_low, 1)
                if t % 4 == 0 and 0 <= (hd := t // 4) < MEM_HEADS:
                    need(e, kxs, 2 * hd + 2)
                    e.tensor_tensor(vx[hd % 2][:, 1, :, :], vmem[:, :, hd * MHD:(hd + 1) * MHD],
                                    vx[hd % 2][:, 0, :, :].bitcast(F32), ALU.subtract).then_inc(kxl, 1)
                if 0 <= (w := t - 5) < 16:
                    need(e, xo_high, w + 1)
                    dst = h[:, :, 2 * (w // 4):2 * (w // 4) + 2, w % 4 * 256:(w % 4 + 1) * 256]
                    e.tensor_tensor(dst[:, 1, :, :], psO(w).rearrange("p (d q) -> p d q", d=2),
                                    dst[:, 0, :, :].bitcast(F32), ALU.subtract).then_inc(xo_low, 1)

            with e.Fori(0, O_BLOCKS - 1) as n:
                for r in range(16):
                    add(O0 + n, O_D + n, r, 1.0)
            boundary(3, FFN2 - 1, O_D + DT - 1, 1.0, 3)

            ffn(FFN2, FT, FFN2_T, FFN2_D)
            for r in range(16):
                add(BLOCKS - 1, FFN2_D + FT - 1, r, 0.5)
            need(e, x_added, 16 * (FFN2_D + FT))

            def outputs(half, tiles):
                need(e, rstd_made, 8 + half + 1)
                for k in tiles:
                    e.scalar_tensor_tensor(out=qkv[:, k, hs(half)], in0=x[:, k, hs(half)],
                                           scalar=gn[:, 5, k:k + 1], in1=rstd[:, hs(half)],
                                           op0=ALU.mult, op1=ALU.mult).then_inc(outs, 1)

            one_rstd(4, 0)
            outputs(0, (0, 1, 2, 3))
            one_rstd(4, 1)
            outputs(1, (0, 1, 2, 3, 4, 5))


def launch_arrays(x, mem, positions, rel_bias, ffn1_norm, ffn1_w_gu, ffn1_w_down, mix_norm, w_in, sinks, conv_w,
                  w_out, xattn_norm, mem_norm, xattn_wq, xattn_wkv, xattn_wo, ffn2_norm, ffn2_w_gu, ffn2_w_down,
                  final_norm):
    group = HEADS // KVH
    order = [2 * (j // group) * group + half * group + j % group for j in range(DT) for half in range(2)]
    chan = np.concatenate([np.arange(o * HD, (o + 1) * HD) for o in order])

    def tiles(a):
        return a.reshape(-1, P, a.shape[1]).transpose(1, 0, 2)

    def columns(w):
        return w.reshape(DT, P, -1, P).transpose(2, 1, 0, 3).reshape(-1, P, D)

    def rows(w):
        return w.reshape(-1, P, D)

    def ffn(gu, down):
        gate, up, dn = columns(gu[:, :F]), columns(gu[:, F:]), rows(down)
        seq = [gate[0:1], up[0:1]]
        for t in range(1, FT):
            seq += [gate[t:t + 1], dn[t - 1:t], up[t:t + 1]]
        return seq + [dn[FT - 1:FT]]

    w = w_in[0]
    at = np.cumsum([0, D, KVH * HD, KVH * HD, D, D, D, D, D])
    q, k, v, c, b, u, ga, gc = (w[:, at[n]:at[n + 1]] for n in range(8))
    c, b, u, ga, gc = (columns(m[:, chan]) for m in (c, b, u, ga, gc))
    wo = rows(w_out[0][chan, :])
    blocks = [columns(xattn_wkv[0])]
    blocks += ffn(ffn1_w_gu[0], ffn1_w_down[0])
    blocks += [columns(q[:, chan]), columns(k), columns(v)]
    for t in range(DT):
        one = slice(t, t + 1)
        blocks += [c[one], u[one]] + ([wo[t - 1:t]] if t else []) + [b[one], gc[one], ga[one]]
    blocks += [wo[DT - 1:DT], columns(xattn_wq[0]), rows(xattn_wo[0])]
    blocks += ffn(ffn2_w_gu[0], ffn2_w_down[0])

    onehot = np.zeros((BUCKETS + 1, RUN), np.float32)
    for m in range(RUN):
        rel = 2 * P - m
        onehot[bucket(rel) if 0 <= rel < WINDOW else BUCKETS, m] = 1.0

    gains = np.stack([g.reshape(DT, P).T for g in
                      (ffn1_norm[0], mix_norm[0], xattn_norm[0], ffn2_norm[0], mem_norm[0], final_norm)], 1)
    return {
        "xT": tiles(x[0].T), "memT": tiles(mem[0].T), "weights": np.concatenate(blocks, 0), "gains": gains,
        "conv_w": conv_w[0][:, chan].reshape(3, DT, P).transpose(2, 1, 0), "table": rel_bias[:, order],
        "onehot": onehot, "sinks": sinks[:, order], "positions": positions,
    }


def bucket(n):
    return int(np.searchsorted(STARTS, n, side="right")) - 1


STARTS = list(range(16)) + [int(np.ceil(16 * (MAX_DIST / 16) ** (n / 16) - 1e-9)) for n in range(16)]


def kernel(**inputs):
    import concourse.bacc as bacc
    from concourse.bass_utils import run_bass_kernel_spmd

    nc = bacc.Bacc("TRN2", target_bir_lowering=False, num_devices=1)
    arrays, args = {}, {}
    for name, a in launch_arrays(**{k: np.asarray(v) for k, v in inputs.items()}).items():
        a = np.ascontiguousarray(a)
        arrays[f"in_{name}"] = a
        args[name] = nc.dram_tensor(f"in_{name}", a.shape, mybir.dt.from_np(a.dtype), kind="ExternalInput").ap()
    out = nc.dram_tensor("out_T", (P, DT, S), F32, kind="ExternalOutput").ap()
    build(nc, *[args[n] for n in ("xT", "memT", "weights", "gains", "conv_w", "table", "onehot", "sinks",
                                  "positions")], out)
    got = run_bass_kernel_spmd(nc, [arrays], core_ids=[0]).results[0]["out_T"]
    return np.asarray(got).transpose(1, 0, 2).reshape(D, S).T[None]
```
